# Optimizing a Trainium2 kernel written in Bass

```python
import jax, jax.numpy as jnp
from jax import lax
import numpy as np

D_MODEL = 1024
BATCH = 1
SEQ = 1024
DEPTH = 1

HEAD_DIM = 64
ATTN_HEADS = 8
ATTN_KV_HEADS = 2
ATTN_GROUP = ATTN_HEADS // ATTN_KV_HEADS
WINDOW = 128
ATTN_WIDTH = ATTN_HEADS * HEAD_DIM
ATTN_KV_WIDTH = ATTN_KV_HEADS * HEAD_DIM
RET_HEADS = 4
RET_HEAD_DIM = 128
RET_WIDTH = RET_HEADS * RET_HEAD_DIM
RET_CHUNK = 128
PEER_HEADS = 8
PEER_N_KEYS = 128
PEER_N_EXPERTS = PEER_N_KEYS * PEER_N_KEYS
PEER_QUERY_DIM = 256
PEER_HALF_DIM = PEER_QUERY_DIM // 2
PEER_TOPK = 16
PEER_BLOCK = 128
DEEPNORM_ALPHA = (2 * DEPTH) ** 0.25
DEEPNORM_BETA = (8 * DEPTH) ** -0.25
LN_EPS = 1e-5
GN_EPS = 1e-5
IN_SPLITS = (ATTN_WIDTH, ATTN_KV_WIDTH, ATTN_KV_WIDTH, RET_WIDTH, RET_WIDTH, RET_WIDTH, RET_WIDTH, D_MODEL, D_MODEL)
IN_WIDTH = sum(IN_SPLITS)
V_COLUMN_GROUPS = (2, 5)

kernel_name = "hybrid_swa_retention_peer_deepnorm"

def layer_norm(x, gain, bias):
    xf = x.astype(jnp.float32)
    mu = jnp.mean(xf, axis=-1, keepdims=True)
    var = jnp.mean(jnp.square(xf - mu), axis=-1, keepdims=True)
    y = (xf - mu) * lax.rsqrt(var + LN_EPS) * gain.astype(jnp.float32) + bias.astype(jnp.float32)
    return y.astype(x.dtype)

def alibi_slopes(n_heads):
    return 2.0 ** (-8.0 * jnp.arange(1, n_heads + 1, dtype=jnp.float32) / n_heads)

def sliding_window_attention(q, k, v, sinks):
    B, S = q.shape[:2]
    nb = S // WINDOW
    qb = q.reshape(B, nb, WINDOW, ATTN_KV_HEADS, ATTN_GROUP, HEAD_DIM)
    kb = k.reshape(B, nb, WINDOW, ATTN_KV_HEADS, HEAD_DIM)
    vb = v.reshape(B, nb, WINDOW, ATTN_KV_HEADS, HEAD_DIM)
    pad = ((0, 0), (1, 0), (0, 0), (0, 0), (0, 0))
    kk = jnp.concatenate([jnp.pad(kb, pad)[:, :-1], kb], axis=2)
    vv = jnp.concatenate([jnp.pad(vb, pad)[:, :-1], vb], axis=2)
    scores = jnp.einsum("bnqkgd,bnskd->bnkgqs", qb, kk).astype(jnp.float32)
    dist = (jnp.arange(WINDOW)[:, None] + WINDOW) - jnp.arange(2 * WINDOW)[None, :]
    in_band = (dist >= 0) & (dist < WINDOW)
    has_prev = (jnp.arange(nb)[:, None, None] > 0) | (jnp.arange(2 * WINDOW)[None, None, :] >= WINDOW)
    valid = in_band[None] & has_prev
    slopes = alibi_slopes(ATTN_HEADS).reshape(ATTN_KV_HEADS, ATTN_GROUP, 1, 1)
    scores = scores - slopes * dist.astype(jnp.float32)
    scores = jnp.where(valid[None, :, None, None], scores, -jnp.inf)
    sink = jnp.broadcast_to(sinks.astype(jnp.float32).reshape(ATTN_KV_HEADS, ATTN_GROUP, 1, 1),
                            scores.shape[:-1] + (1,))
    probs = jax.nn.softmax(jnp.concatenate([scores, sink], axis=-1), axis=-1)[..., :-1]
    out = jnp.einsum("bnkgqs,bnskd->bnqkgd", probs.astype(v.dtype), vv)
    return out.reshape(B, S, ATTN_WIDTH)

def retention_chunkwise(q, k, v):
    B, S, H, _ = q.shape
    Dv = v.shape[-1]
    nc = S // RET_CHUNK
    f32 = jnp.float32
    log_gamma = jnp.log1p(-(2.0 ** (-5.0 - jnp.arange(H, dtype=f32))))
    pos = jnp.arange(RET_CHUNK, dtype=f32)
    diff = pos[:, None] - pos[None, :]
    inner_decay = jnp.where(diff >= 0, jnp.exp(jnp.maximum(diff, 0.0) * log_gamma[:, None, None]), 0.0)
    k_decay = jnp.exp((RET_CHUNK - 1.0 - pos) * log_gamma[:, None])
    q_decay = jnp.exp((pos + 1.0) * log_gamma[:, None])
    chunk_decay = jnp.exp(RET_CHUNK * log_gamma)

    def to_chunks(t):
        return t.astype(f32).reshape(B, nc, RET_CHUNK, H, t.shape[-1]).transpose(1, 0, 3, 2, 4)

    qc, kc, vc = to_chunks(q), to_chunks(k), to_chunks(v)
    inner = jnp.einsum("nbhij,nbhje->nbhie", jnp.einsum("nbhid,nbhjd->nbhij", qc, kc) * inner_decay, vc)
    chunk_kv = jnp.einsum("nbhjd,hj,nbhje->nbhde", kc, k_decay, vc)

    def step(state, kv):
        return chunk_decay[None, :, None, None] * state + kv, state

    _, prev = lax.scan(step, jnp.zeros(chunk_kv.shape[1:], f32), chunk_kv)
    cross = jnp.einsum("nbhid,nbhde->nbhie", qc, prev) * q_decay[:, :, None]
    return (inner + cross).transpose(1, 0, 3, 2, 4).reshape(B, S, H, Dv)

def head_group_norm(y, gain):
    B, S = y.shape[:2]
    mu = jnp.mean(y, axis=-1, keepdims=True)
    var = jnp.mean(jnp.square(y - mu), axis=-1, keepdims=True)
    return ((y - mu) * lax.rsqrt(var + GN_EPS)).reshape(B, S, RET_WIDTH) * gain.astype(jnp.float32)

def peer(x, w_query, sub_keys, expert_down, expert_up):
    B, S, D = x.shape
    T = B * S
    xt = x.reshape(T, D)
    q = (xt @ w_query).reshape(T, PEER_HEADS, 2, PEER_HALF_DIM)
    half_scores = jnp.einsum("thpd,pnd->thpn", q, sub_keys).astype(jnp.float32)
    half_vals, half_idx = lax.top_k(half_scores, PEER_TOPK)
    n_cand = PEER_TOPK * PEER_TOPK
    cand_scores = (half_vals[:, :, 0, :, None] + half_vals[:, :, 1, None, :]).reshape(T, PEER_HEADS, n_cand)
    cand_idx = (half_idx[:, :, 0, :, None] * PEER_N_KEYS + half_idx[:, :, 1, None, :]).reshape(T, PEER_HEADS, n_cand)
    top_scores, top_pos = lax.top_k(cand_scores, PEER_TOPK)
    experts = jnp.take_along_axis(cand_idx, top_pos, axis=-1)
    gates = jax.nn.softmax(top_scores, axis=-1).astype(x.dtype)
    nblk = T // PEER_BLOCK

    def block(args):
        xb, eb, gb = args
        down = jnp.take(expert_down, eb, axis=0)
        up = jnp.take(expert_up, eb, axis=0)
        act = jax.nn.gelu(jnp.einsum("phkd,pd->phk", down, xb), approximate=False)
        return jnp.einsum("phk,phkd->pd", gb * act, up)

    out = lax.map(block, (xt.reshape(nblk, PEER_BLOCK, D),
                          experts.reshape(nblk, PEER_BLOCK, PEER_HEADS, PEER_TOPK),
                          gates.reshape(nblk, PEER_BLOCK, PEER_HEADS, PEER_TOPK)))
    return out.reshape(B, S, D)

def setup_inputs(seed: int = 0) -> dict:
    key = jax.random.key(seed)
    ks = jax.random.split(key, 16)
    f32 = jnp.float32

    def normal(k, shape, scale):
        return jax.random.normal(k, shape, f32) * scale

    col_scale = np.concatenate([np.full((w,), DEEPNORM_BETA if i in V_COLUMN_GROUPS else 1.0, np.float32)
                                for i, w in enumerate(IN_SPLITS)])
    return {
        "x": normal(ks[0], (BATCH, SEQ, D_MODEL), 1.0),
        "w_in": normal(ks[1], (DEPTH, D_MODEL, IN_WIDTH), D_MODEL ** -0.5) * jnp.asarray(col_scale),
        "attn_sinks": normal(ks[2], (DEPTH, ATTN_HEADS), 0.5),
        "ret_gn_gain": 1.0 + normal(ks[3], (DEPTH, RET_WIDTH), 0.02),
        "w_attn_branch": normal(ks[4], (DEPTH, ATTN_WIDTH, D_MODEL), DEEPNORM_BETA * ATTN_WIDTH ** -0.5),
        "w_ret_branch": normal(ks[5], (DEPTH, RET_WIDTH, D_MODEL), DEEPNORM_BETA * RET_WIDTH ** -0.5),
        "w_out": normal(ks[6], (DEPTH, D_MODEL, D_MODEL), DEEPNORM_BETA * D_MODEL ** -0.5),
        "ln_mix_gain": 1.0 + normal(ks[7], (DEPTH, D_MODEL), 0.02),
        "ln_mix_bias": normal(ks[8], (DEPTH, D_MODEL), 0.02),
        "w_peer_query": normal(ks[9], (DEPTH, D_MODEL, PEER_HEADS * PEER_QUERY_DIM), D_MODEL ** -0.5),
        "peer_sub_keys": normal(ks[10], (DEPTH, 2, PEER_N_KEYS, PEER_HALF_DIM), PEER_HALF_DIM ** -0.5),
        "peer_down": normal(ks[11], (DEPTH, PEER_N_EXPERTS, D_MODEL), D_MODEL ** -0.5),
        "peer_up": normal(ks[12], (DEPTH, PEER_N_EXPERTS, D_MODEL), DEEPNORM_BETA),
        "ln_ffn_gain": 1.0 + normal(ks[13], (DEPTH, D_MODEL), 0.02),
        "ln_ffn_bias": normal(ks[14], (DEPTH, D_MODEL), 0.02),
    }

def reference(x, w_in, attn_sinks, ret_gn_gain, w_attn_branch, w_ret_branch, w_out, ln_mix_gain,
              ln_mix_bias, w_peer_query, peer_sub_keys, peer_down, peer_up, ln_ffn_gain, ln_ffn_bias):
    B, S, _ = x.shape
    offsets = np.cumsum(IN_SPLITS)[:-1].tolist()
    for l in range(DEPTH):
        h = x @ w_in[l]
        q_a, k_a, v_a, q_r, k_r, v_r, g_r, gate_a, gate_b = jnp.split(h, offsets, axis=-1)
        attn = sliding_window_attention(
            q_a.reshape(B, S, ATTN_HEADS, HEAD_DIM) * HEAD_DIM ** -0.5,
            k_a.reshape(B, S, ATTN_KV_HEADS, HEAD_DIM),
            v_a.reshape(B, S, ATTN_KV_HEADS, HEAD_DIM),
            attn_sinks[l])
        ret = retention_chunkwise(
            q_r.reshape(B, S, RET_HEADS, RET_HEAD_DIM) * RET_HEAD_DIM ** -0.5,
            k_r.reshape(B, S, RET_HEADS, RET_HEAD_DIM),
            v_r.reshape(B, S, RET_HEADS, RET_HEAD_DIM))
        ret = (head_group_norm(ret, ret_gn_gain[l]) * jax.nn.silu(g_r.astype(jnp.float32))).astype(x.dtype)
        merged = (jax.nn.sigmoid(gate_a) * (attn @ w_attn_branch[l])
                  + jax.nn.sigmoid(gate_b) * (ret @ w_ret_branch[l]))
        x = layer_norm(DEEPNORM_ALPHA * x + merged @ w_out[l], ln_mix_gain[l], ln_mix_bias[l])
        y = peer(x, w_peer_query[l], peer_sub_keys[l], peer_down[l], peer_up[l])
        x = layer_norm(DEEPNORM_ALPHA * x + y, ln_ffn_gain[l], ln_ffn_bias[l])
    return x


_drawn_inputs = setup_inputs


def setup_inputs(seed=0):
    import zlib

    import numpy as np

    out = dict(_drawn_inputs(seed))
    spreads = {}
    factors = {'attn_sinks': 4.683, 'ret_gn_gain': 5.16, 'ln_ffn_gain': 2.741, 'ln_ffn_bias': 2.873}
    for name, (base, spread) in spreads.items():
        noise = np.random.default_rng([zlib.crc32(name.encode()), seed]).standard_normal(out[name].shape)
        drawn = base * np.exp(spread * noise) if base else spread * noise
        out[name] = __import__('jax').numpy.asarray(drawn.astype(out[name].dtype))
    for name, factor in factors.items():
        out[name] = (out[name] * factor).astype(out[name].dtype)
    return out
```

```python
from contextlib import ExitStack

import concourse.bass as bass
import numpy as np
from concourse import mybir

F32 = mybir.dt.float32
U32 = mybir.dt.uint32
ALU = mybir.AluOpType
ACT = mybir.ActivationFunctionType
AX = mybir.AxisListType.X

P = 128
D = 1024
KD = D // P
S = 1024
TILES = 2
NT = TILES * P
BLOCKS = S // NT
HD, KVH, GROUP = 64, 2, 4
AH = KVH * GROUP
RH = 4
PH, TOPK, NK = 8, 16, 128
SLOTS = PH * TOPK
ALPHA = float(2.0 ** 0.25)
EPS = 1e-5
FAR = 1.0e30
LOWEST = -3.0e38

RING = 10
PAIR = 2
GROUPS = TILES * SLOTS // PAIR
TGROUPS = SLOTS // PAIR
_ROUNDS = -(-GROUPS // (RING // PAIR))
_SHORT = _ROUNDS * (RING // PAIR) - GROUPS
PLACE = [j for r in range(_ROUNDS) for j in range(RING // PAIR - ((r + 1) * _SHORT // _ROUNDS > r * _SHORT // _ROUNDS))]
WRING = 3
BANKS = 6

PARTS = (
    [("kv",), ("qa", 0), ("qa", 1), ("scores", 0, 0), ("qr", 0), ("turn", 0, 0), ("scores", 0, 1),
     ("qr", 1), ("pv", 0, 0), ("turn", 0, 1), ("scores", 1, 0), ("kr", 0), ("pv", 0, 1), ("turn", 1, 0),
     ("scores", 1, 1), ("kr", 1), ("pv", 1, 0), ("turn", 1, 1), ("vr", 0), ("pv", 1, 1), ("vr", 1),
     ("gr", 0), ("ret_scores", 0), ("gr", 1), ("ret_out", 0), ("gate", 0), ("ret_turn", 0),
     ("ret_scores", 1), ("gate", 1), ("ret_out", 1), ("ret_turn", 1)]
    + [p for m in range(0, KD, 2)
       for p in ([("gate", m), ("gate", m + 1)] if m else []) + [("branch", m), ("branch", m + 1)]]
    + [("out", n) for n in range(4)] + [("norm", 0), ("x1turn", 0), ("norm", 1), ("x1turn", 1)]
    + [p for h in range(PH) for p in (("query", h), ("halves", h))]
    + [("pick", 0, s) for s in range(6)] + [("publish",)]
)
TAIL = tuple(("pick", 1, s) for s in range(6))
PAIRS = [p for p in PARTS if p[0] in ("kv", "qa", "qr", "kr", "vr", "gr", "gate", "out", "query")
         or (p[0] == "branch" and p[1] % 2 == 0)]
PAIR_AT = {p: n for n, p in enumerate(PAIRS)}
for _m in range(1, KD, 2):
    PAIR_AT[("branch", _m)] = PAIR_AT[("branch", _m - 1)]
USES = []
for _p in PARTS:
    _n = {"scores": 2, "turn": 2, "ret_scores": 2, "ret_out": 2, "x1turn": 2, "norm": 0, "pick": 0, "publish": 0}
    USES += [(*_p, i) for i in range(_n.get(_p[0], 1))]
USE_AT = {u: n for n, u in enumerate(USES)}
LAST_USE = [USE_AT[(p[0], p[1] + 1, 0) if p[0] == "branch" else (*p, 0)] for p in PAIRS]
BANK_USES = [len(range(b, len(USES), BANKS)) for b in range(BANKS)]
BUF_PAIRS = [len(range(b, len(PAIRS), WRING)) for b in range(WRING)]

C_IDENT, C_DIST, C_RMASK, C_QDEC, C_KDEC, C_IOTA, C_END = np.cumsum([0, P, 2 * P, RH * P, RH * P, RH, TOPK]).tolist()
R_MG, R_MB, R_FG, R_FB, R_GN, R_SINK, R_END = np.cumsum([0, D, D, D, D, RH * P, AH]).tolist()


def log_gammas():
    return np.log1p(-(2.0 ** (-5.0 - np.arange(RH, dtype=np.float32)))).astype(np.float32)


def constants():
    c = np.zeros((P, C_END), np.float32)
    c[:, C_IDENT:C_DIST] = np.eye(P)
    dist = (np.arange(P)[:, None] + P) - np.arange(2 * P)[None, :]
    c[:, C_DIST:C_RMASK] = np.where((dist >= 0) & (dist < P), dist, FAR)
    lg = log_gammas()
    pos = np.arange(P, dtype=np.float32)
    for h in range(RH):
        diff = pos[None, :] - pos[:, None]
        c[:, C_RMASK + h * P:C_RMASK + (h + 1) * P] = np.where(diff >= 0, np.exp(np.maximum(diff, 0) * lg[h]), 0)
        c[:, C_QDEC + h * P:C_QDEC + (h + 1) * P] = np.exp((pos + 1) * lg[h])[None, :]
        c[:, C_KDEC + h] = np.exp((P - 1 - pos) * lg[h])
    c[:, C_IOTA:C_END] = np.arange(TOPK)[None, :]
    return c


def build(nc, xT_d, xn_d, w_d, keys_d, const_d, par_d, rows_d, out_d):
    slopes = [float(2.0 ** (-8.0 * (h + 1) / AH)) for h in range(AH)]
    chunk_decay = [float(np.exp(np.float32(P) * g)) for g in log_gammas()]
    with ExitStack() as ctx:
        def sb(name, shape, dt=F32):
            return ctx.enter_context(nc.sbuf_tensor(name, shape, dt))

        def sem(name):
            return ctx.enter_context(nc.semaphore(name))

        ps = ctx.enter_context(nc.psum_tensor("ps", [P, 8, 512], F32))
        acc = ps[:, BANKS:8, :].rearrange("p a b -> p (a b)")

        const = sb("const", [P, C_END])
        ident = const[:, C_IDENT:C_DIST]
        dist = const[:, C_DIST:C_RMASK]
        rmask = const[:, C_RMASK:C_QDEC]
        qdec = const[:, C_QDEC:C_KDEC].rearrange("p (h i) -> p h i", h=RH)
        kdec = const[:, C_KDEC:C_IOTA]
        iota = const[:, C_IOTA:C_END]
        par = sb("par", [P, R_END])
        keys = sb("keys", [P, 2, NK])
        weights = sb("weights", [P, WRING, 2, KD, P])
        rows = sb("rows", [P, RING, 2, D])
        xT = sb("xT", [P, KD, NT])
        x1n = sb("x1n", [P, TILES, D])
        qrT = x1n[:, 0, :].rearrange("p (h n) -> p h n", h=RH)
        krT = x1n[:, 1, :].rearrange("p (h n) -> p h n", h=RH)
        kT = sb("kT", [P, 3, P])
        v = sb("v", [P, 3, P])
        vr = sb("vr", [P, TILES, RH * P])
        gates = sb("gates", [P, 2, 2, NT])
        pick8k = sb("pick8k", [P, 2, D])
        probs = pick8k[:, 0, :].rearrange("p (j s) -> p j s", j=GROUP)
        probsT = pick8k[:, 1, :].rearrange("p (k n) -> p k n", k=2)
        cand = pick8k[:, :, :].rearrange("p a b -> p (a b)").rearrange("p (h c) -> p h c", h=PH)
        attnT = sb("attnT", [P, GROUP, NT])
        retT = pick8k[:, 1, :].rearrange("p (h n) -> p h n", h=RH)
        maskedT = sb("maskedT", [P, RH * P])
        kd = sb("kd", [P, RH * P])
        qd = sb("qd", [P, RH, P])
        ret = sb("ret", [P, RH * P])
        state = sb("state", [P, RH * P])
        merged = sb("merged", [P, KD, NT])
        qT = merged[:, 0:GROUP, :]
        swish = merged[:, GROUP:, :].rearrange("p a b -> p (a b)").rearrange("p (t n) -> p t n", t=TILES)
        onehot = merged[:, :, :].rearrange("p a b -> p (a b)").rearrange("p (s a) -> p s a", a=TOPK)
        queryT = attnT[:, 0:2, :]
        small = sb("small", [P, 32])
        stats = sb("stats", [P, RH, 6])
        mv = sb("mv", [P, RH, 2])
        rstd = sb("rstd", [P, RH])
        variance = sb("variance", [P, RH])
        roottmp = sb("roottmp", [P, RH])
        rest = vr[:, 0, :].rearrange("p (a c) -> p a c", a=2)
        val = maskedT[:, :].rearrange("p (t a h k) -> p t a h k", t=TILES, a=2, h=PH)
        idx = kd[:, :].bitcast(U32).rearrange("p (t a h k) -> p t a h k", t=TILES, a=2, h=PH)
        idxf, posf = (qd[:, 2 * i:2 * i + 2, :] for i in range(2))
        part_e = ret[:, 0:2 * SLOTS].rearrange("p (a s) -> p a s", a=2)
        posu = ret[:, 2 * SLOTS:].bitcast(U32).rearrange("p (a s) -> p a s", a=2)
        topv = sb("topv", [P, PH, TOPK])
        topp = sb("topp", [P, SLOTS], U32)
        gsum = sb("gsum", [P, 2, PH])
        expert_next = sb("expert_next", [P, TILES, SLOTS], U32)
        gate_next = sb("gate_next", [P, TILES, SLOTS])
        expert = sb("expert", [P, TILES, SLOTS], U32)
        gate = sb("gate", [P, TILES, SLOTS])
        x1 = sb("x1", [P, TILES, D])
        hdot = sb("hdot", [P, 2, PAIR])
        hact = sb("hact", [P, 2, PAIR])
        diag = sb("diag", [P, 2, PAIR, P])
        y = sb("y", [P, D])
        fstats = sb("fstats", [P, 2, 6])
        fmv = sb("fmv", [P, 2])
        frstd = sb("frstd", [P, 1])

        const_landed = sem("const_landed")
        landed = [sem(f"weights_landed{b}") for b in range(WRING)]
        xT_landed, xn_landed = sem("xT_landed"), sem("xn_landed")
        bank_full = sem("bank_full")
        emptied = [sem(f"bank_emptied{b}") for b in range(BANKS)]
        state_zeroed = sem("state_zeroed")
        max_ready, exp_done, probs_ready = sem("max_ready"), sem("exp_done"), sem("probs_ready")
        qd_ready, ret_ready, x1_ready = sem("qd_ready"), sem("ret_ready"), sem("x1_ready")
        gdiff_ready, gexp_done = sem("gdiff_ready"), sem("gate_exp_done")
        swish_exp = sem("swish_exp")
        mix_step, fin_step = sem("mix_step"), sem("fin_step")
        published = sem("published")
        gathered = [sem(f"gathered{b}") for b in range(RING)]
        dots_done, gelu_done, diag_ready = sem("dots_done"), sem("gelu_done"), sem("diag_ready")
        up_done, acc_read = sem("up_done"), sem("acc_read")
        out_ready, stored = sem("out_ready"), sem("stored")
        passed = [sem("vector_passed"), sem("pool_passed")]
        pool_engine = nc.gpsimd

        def at(b, per, n):
            return b * per + n

        def started(b):
            return not isinstance(b, int) or b > 0

        def filled(b, *use):
            return at(b, len(USES), USE_AT[use] + 1)

        def bank_no(*use):
            return USE_AT[use] % BANKS

        def bank_of(*use):
            return ps[:, bank_no(*use), :]

        def free(b, *use):
            return at(b, BANK_USES[bank_no(*use)], USE_AT[use] // BANKS + 1)

        def stands(b, *uses):
            last = {bank_no(*u): u for u in sorted(uses, key=USE_AT.get)}
            return [(emptied[n], free(b, *u) + 1) for n, u in last.items()]

        def buffer(g, i):
            return PLACE[g] * PAIR + i

        def arrived(b, g):
            return at(b, 16 * PLACE.count(PLACE[g]), 16 * PLACE[:g + 1].count(PLACE[g]))

        def used_before(b, g):
            n = max([m for m in range(g) if PLACE[m] == PLACE[g]], default=None)
            if n is None:
                return at(b, GROUPS, max(m for m in range(GROUPS) if PLACE[m] == PLACE[g]) + 1 - GROUPS) if started(b) else None
            return at(b, GROUPS, n + 1)

        def settle(eng):
            eng.sem_inc(passed[eng is pool_engine], 1)

        def spread(g, mix, done):
            goal = min(len(PARTS), max(0, g - len(TAIL) + 1) * len(PARTS) // (GROUPS - len(TAIL) - 4))
            while done[0] < goal:
                next(mix)
                done[0] += 1

        block = ctx.enter_context(nc.Block())

        @block.sync
        def _(sp):
            sp.dma_start(const[:, :], const_d).then_inc(const_landed, 16)

            def loads(b):
                if started(b):
                    sp.wait_ge(bank_full, at(b, len(USES), 0))
                sp.dma_start(xT[:, :, :], xT_d[bass.ds(b, 1)].rearrange("b p k n -> (b p) k n")).then_inc(xT_landed, 16)
                for n, pair in enumerate(PAIRS):
                    if n >= WRING:
                        sp.wait_ge(bank_full, at(b, len(USES), LAST_USE[n - WRING] + 1))
                    elif started(b):
                        last = max(m for m in range(len(PAIRS)) if m % WRING == n)
                        sp.wait_ge(bank_full, at(b - 1, len(USES), LAST_USE[last] + 1))
                    sp.dma_start(weights[:, n % WRING].rearrange("p u k c -> p (u k c)"),
                                 w_d[n]).then_inc(landed[n % WRING], 16)
                    if isinstance(b, int) and n == 0:
                        sp.dma_start(par[:, :], par_d).then_inc(const_landed, 16)
                        sp.dma_start(keys[:, :, :], keys_d).then_inc(const_landed, 16)
                    if pair == ("gate", 5):
                        sp.wait_ge(bank_full, filled(b, "ret_turn", 1, 0))
                        sp.dma_start(x1n[:, :, :],
                                     xn_d[bass.ds(b, 1)].rearrange("b p t d -> (b p) t d")).then_inc(xn_landed, 16)

            loads(0)
            with sp.Fori(1, BLOCKS) as b:
                loads(b)

        @block.gpsimd
        def _(pool):
            def gathers(b):
                for g in range(GROUPS):
                    t, s0 = g // TGROUPS, (g % TGROUPS) * PAIR
                    if g % TGROUPS == 0:
                        pool.wait_ge(published, at(b, TILES, t + 1))
                    if used_before(b, g) is not None:
                        pool.wait_ge(up_done, used_before(b, g))
                        settle(pool)
                    for i in range(PAIR):
                        buf = buffer(g, i)
                        pool.indirect_dma_start(
                            out=rows[:, buf].rearrange("p a d -> p (a d)"), out_offset=None, in_=rows_d,
                            in_offset=bass.IndirectOffsetOnAxis(ap=expert[:, t, s0 + i:s0 + i + 1], axis=0),
                        ).then_inc(gathered[buf], 16)

            gathers(0)
            with pool.Fori(1, BLOCKS) as b:
                gathers(b)

        @block.scalar
        def _(act):
            def copy(out, use, b, scale=1.0, part=None):
                act.wait_ge(bank_full, filled(b, *use))
                bank = bank_of(*use)
                act.activation(out, bank if part is None else bank[part], ACT.Copy, scale=scale).then_inc(emptied[bank_no(*use)], 1)

            def mixer(b, parts=PARTS):
                for part in parts:
                    kind, *pos = part
                    if kind == "qa":
                        i = pos[0]
                        if i == 0 and started(b):
                            act.wait_ge(published, at(b, TILES, 0))
                        copy(qT[:, 2 * i:2 * i + 2, :].rearrange("p j n -> p (j n)"), (*part, 0), b, HD ** -0.5)
                    elif kind in ("qr", "kr"):
                        i = pos[0]
                        to = qrT if kind == "qr" else krT
                        copy(to[:, 2 * i:2 * i + 2, :].rearrange("p j n -> p (j n)"), (*part, 0), b,
                             P ** -0.5 if kind == "qr" else 1.0)
                    elif kind == "scores":
                        c, h = pos
                        n = c * KVH + h
                        lo = P if isinstance(b, int) and b == 0 and c == 0 else 0
                        act.wait_ge(max_ready, at(b, 2 * KVH, n + 1))
                        for j in range(GROUP):
                            act.activation(probs[:, j, lo:], probs[:, j, lo:], ACT.Exp, bias=small[:, 4 + j:5 + j],
                                           accum_out=small[:, 12 + j:13 + j])
                        act.activation(small[:, 16:20], small[:, 8:12], ACT.Exp).then_inc(exp_done, 1)
                    elif kind == "turn":
                        c, h = pos
                        for k in range(2):
                            copy(probsT[:, k, :], (*part, k), b)
                    elif kind == "pv":
                        c, h = pos
                        half = slice(HD * h, HD * h + HD)
                        act.wait_ge(bank_full, filled(b, *part, 0))
                        bank = bank_of(*part, 0)
                        act.activation(attnT[half, :, c * P:c * P + P],
                                             bank[half].rearrange("p (j n) -> p j n", j=GROUP), ACT.Copy).then_inc(emptied[bank_no(*part, 0)], 1)
                    elif kind in ("gr", "gate"):
                        n = pos[0]
                        act.wait_ge(bank_full, filled(b, *part, 0))
                        bank = bank_of(*part, 0)
                        if kind == "gate":
                            for bank_emptied, turn in stands(b, ("branch", n - 2, 0) if n >= 2 else ("gr", n, 0)):
                                act.wait_ge(bank_emptied, turn)
                        elif started(b):
                            for bank_emptied, turn in stands(b - 1, ("branch", KD - 2 + n, 0)):
                                act.wait_ge(bank_emptied, turn)
                        ins = act.activation(gates[:, n % 2].rearrange("p a n -> p (a n)"), bank, ACT.Exp, scale=-1.0)
                        if kind == "gate":
                            ins.then_inc(emptied[bank_no(*part, 0)], 1)
                        else:
                            ins.then_inc(swish_exp, 1)
                    elif kind == "ret_turn":
                        c = pos[0]
                        act.wait_ge(bank_full, filled(b, *part, 0))
                        bank = bank_of(*part, 0)
                        act.activation(retT[:, :, c * P:c * P + P],
                                             bank.rearrange("p (h n) -> p h n", h=RH), ACT.Copy).then_inc(emptied[bank_no(*part, 0)], 1)
                    elif kind == "x1turn":
                        t = pos[0]
                        for i in range(2):
                            act.wait_ge(bank_full, filled(b, *part, i))
                            bank = bank_of(*part, i)
                            act.activation(xT[:, 4 * i:4 * i + 4, t * P:t * P + P],
                                                 bank.rearrange("p (k n) -> p k n", k=4), ACT.Copy).then_inc(emptied[bank_no(*part, i)], 1)
                    elif kind == "query":
                        copy(queryT[:, :, :].rearrange("p a n -> p (a n)"), (*part, 0), b)
                    elif kind == "pick" and pos[1] == 5:
                        t = pos[0]
                        act.wait_ge(gdiff_ready, at(b, TILES, t + 1))
                        act.activation(topv[:, :, :], topv[:, :, :], ACT.Exp).then_inc(gexp_done, 1)
                    yield

            def peer(b, mix):
                done = [0]
                tail = mixer(b, TAIL)
                for g in range(GROUPS):
                    act.wait_ge(dots_done, at(b, GROUPS, g + 1))
                    if g > 1:
                        act.wait_ge(diag_ready, at(b, GROUPS, g - 1))
                    act.activation(hact[:, g % 2, :], hdot[:, g % 2, :], ACT.Gelu).then_inc(gelu_done, 1)
                    if g < len(TAIL):
                        next(tail)
                    if mix:
                        spread(g, mix, done)
                    if g == TGROUPS + 12:
                        store(b, 0)
                store(b, 1)

            def store(b, t):
                act.wait_ge(out_ready, at(b, TILES, t + 1))
                act.dma_start(out_d[bass.ds(b, 1), t].rearrange("b p d -> (b p) d"), y[:, :]).then_inc(stored, 16)

            act.sem_inc(stored, 16)
            act.wait_ge(const_landed, 48)
            for _ in mixer(0):
                pass
            with act.Fori(0, BLOCKS - 1) as b:
                peer(b, mixer(b + 1))
            peer(BLOCKS - 1, None)
            act.wait_ge(stored, 16 * (TILES * BLOCKS + 1))

        @block.tensor
        def _(pe):
            def mixer(b, parts=PARTS):
                for part in parts:
                    kind, *pos = part
                    if part in PAIR_AT:
                        n = PAIR_AT[part]
                        if kind != "branch" or pos[0] % 2 == 0:
                            pe.wait_ge(landed[n % WRING], at(b, 16 * BUF_PAIRS[n % WRING], 16 * (n // WRING + 1)))
                        w = weights[:, n % WRING]
                    if part == ("kv",):
                        pe.wait_ge(xT_landed, at(b, 16, 16))
                    last = None
                    if kind in ("qa", "qr", "kr", "gate", "query", "kv", "vr", "gr"):
                        if part == ("query", 0):
                            for bank_emptied, turn in stands(b, *(("x1turn", t, i) for t in range(TILES) for i in range(2))):
                                pe.wait_ge(bank_emptied, turn)
                        pe.wait_ge(emptied[bank_no(*part, 0)], free(b, *part, 0))
                        bank = bank_of(*part, 0)
                        for u in range(2):
                            if kind in ("vr", "gr") or (kind == "kv" and u == 1):
                                for t in range(TILES):
                                    at_col = TILES + t if kind == "kv" else t * 2 + u
                                    o = bank[:, at_col * P:(at_col + 1) * P]
                                    for k in range(KD):
                                        last = pe.matmul(o, xT[:, k, t * P:t * P + P], w[:, u, k, :],
                                                         start=k == 0, stop=k == KD - 1)
                            else:
                                for k in range(KD):
                                    last = pe.matmul(bank[:, u * NT:u * NT + NT], w[:, u, k, :], xT[:, k, :],
                                                     start=k == 0, stop=k == KD - 1)
                        last.then_inc(bank_full, 1)
                    elif kind == "scores":
                        c, h = pos
                        if part == ("scores", 0, 0):
                            for bank_emptied, turn in stands(b, ("kv", 0), ("qa", 0, 0), ("qa", 1, 0)):
                                pe.wait_ge(bank_emptied, turn)
                        half = slice(HD * h, HD * h + HD)
                        for i in range(2):
                            pe.wait_ge(emptied[bank_no(*part, i)], free(b, *part, i))
                            bank = bank_of(*part, i)
                            for j in range(2):
                                last = pe.matmul(bank[:, j * NT:(j + 1) * NT], qT[half, 2 * i + j, c * P:c * P + P],
                                                 kT[half, c:c + 2, :].rearrange("p a n -> p (a n)"),
                                                 start=True, stop=True)
                            last.then_inc(bank_full, 1)
                    elif kind == "turn":
                        c, h = pos
                        pe.wait_ge(probs_ready, at(b, 2 * KVH, c * KVH + h + 1))
                        for k in range(2):
                            pe.wait_ge(emptied[bank_no(*part, k)], free(b, *part, k))
                            bank = bank_of(*part, k)
                            for j in range(GROUP):
                                last = pe.transpose(bank[:, j * P:j * P + P], probs[:, j, k * P:k * P + P], ident)
                            last.then_inc(bank_full, 1)
                    elif kind == "pv":
                        c, h = pos
                        half = slice(HD * h, HD * h + HD)
                        for bank_emptied, turn in stands(b, ("turn", c, h, 0), ("turn", c, h, 1)):
                            pe.wait_ge(bank_emptied, turn)
                        pe.wait_ge(emptied[bank_no(*part, 0)], free(b, *part, 0))
                        bank = bank_of(*part, 0)
                        for k in range(2):
                            last = pe.matmul(bank[half], v[:, c + k, half], probsT[:, k, :],
                                             start=k == 0, stop=k == 1)
                        last.then_inc(bank_full, 1)
                    elif kind == "ret_scores":
                        c = pos[0]
                        if c == 0:
                            for bank_emptied, turn in stands(b, *((m, i, 0) for m in ("qr", "kr") for i in range(2))):
                                pe.wait_ge(bank_emptied, turn)
                        tok = slice(c * P, c * P + P)
                        pe.wait_ge(emptied[bank_no(*part, 0)], free(b, *part, 0))
                        bank = bank_of(*part, 0)
                        for h in range(RH):
                            last = pe.matmul(bank[:, h * P:h * P + P], krT[:, h, tok], qrT[:, h, tok],
                                             start=True, stop=True)
                        last.then_inc(bank_full, 1)
                        pe.wait_ge(emptied[bank_no(*part, 1)], free(b, *part, 1))
                        bank = bank_of(*part, 1)
                        for h in range(RH):
                            last = pe.transpose(bank[:, h * P:h * P + P], krT[:, h, tok], ident)
                        last.then_inc(bank_full, 1)
                    elif kind == "ret_out":
                        c = pos[0]
                        if isinstance(b, int) and c == 0:
                            pe.wait_ge(state_zeroed, 1)
                        for bank_emptied, turn in stands(b, *((("vr", 0, 0), ("vr", 1, 0)) if c == 0 else (("ret_out", 0, 1),)), ("ret_scores", c, 0), ("ret_scores", c, 1)):
                            pe.wait_ge(bank_emptied, turn)
                        pe.wait_ge(qd_ready, at(b, TILES, c + 1))
                        pe.wait_ge(emptied[bank_no(*part, 0)], free(b, *part, 0))
                        bank = bank_of(*part, 0)
                        for h in range(RH):
                            o = slice(h * P, h * P + P)
                            pe.matmul(bank[:, o], maskedT[:, o], vr[:, c, o], start=True, stop=False)
                            last = pe.matmul(bank[:, o], qd[:, h, :], state[:, o], start=False, stop=True)
                        last.then_inc(bank_full, 1)
                        pe.wait_ge(emptied[bank_no(*part, 1)], free(b, *part, 1))
                        bank = bank_of(*part, 1)
                        for h in range(RH):
                            o = slice(h * P, h * P + P)
                            last = pe.matmul(bank[:, o], kd[:, o], vr[:, c, o], start=True, stop=True)
                        last.then_inc(bank_full, 1)
                    elif kind == "ret_turn":
                        c = pos[0]
                        pe.wait_ge(ret_ready, at(b, TILES, c + 1))
                        pe.wait_ge(emptied[bank_no(*part, 0)], free(b, *part, 0))
                        bank = bank_of(*part, 0)
                        for h in range(RH):
                            last = pe.transpose(bank[:, h * P:h * P + P], ret[:, h * P:h * P + P], ident)
                        last.then_inc(bank_full, 1)
                    elif kind == "branch":
                        m = pos[0]
                        if m == 0:
                            for bank_emptied, turn in stands(b, *(("pv", c, h, 0) for c in range(TILES) for h in range(KVH)), *(("ret_turn", c, 0) for c in range(TILES))):
                                pe.wait_ge(bank_emptied, turn)
                        pe.wait_ge(emptied[bank_no(*part, 0)], free(b, *part, 0))
                        bank = bank_of(*part, 0)
                        for side, src in enumerate((attnT, retT)):
                            for k in range(4):
                                last = pe.matmul(bank[:, side * NT:side * NT + NT], w[:, m % 2, side * 4 + k, :],
                                                 src[:, k, :], start=k == 0, stop=k == 3)
                        last.then_inc(bank_full, 1)
                    elif kind == "out":
                        if pos[0] == 0:
                            for bank_emptied, turn in stands(b, *(("branch", m, 0) for m in range(KD))):
                                pe.wait_ge(bank_emptied, turn)
                        pe.wait_ge(emptied[bank_no(*part, 0)], free(b, *part, 0))
                        bank = bank_of(*part, 0)
                        for u in range(2):
                            for t in range(TILES):
                                o = bank[:, (t * 2 + u) * P:(t * 2 + u + 1) * P]
                                for k in range(KD):
                                    last = pe.matmul(o, merged[:, k, t * P:t * P + P], w[:, u, k, :],
                                                     start=k == 0, stop=k == KD - 1)
                        last.then_inc(bank_full, 1)
                    elif kind == "x1turn":
                        t = pos[0]
                        pe.wait_ge(x1_ready, at(b, TILES, t + 1))
                        for i in range(2):
                            pe.wait_ge(emptied[bank_no(*part, i)], free(b, *part, i))
                            bank = bank_of(*part, i)
                            for k in range(4):
                                last = pe.transpose(bank[:, k * P:k * P + P],
                                                    x1n[:, t, (4 * i + k) * P:(4 * i + k + 1) * P], ident)
                            last.then_inc(bank_full, 1)
                    elif kind == "halves":
                        h = pos[0]
                        for bank_emptied, turn in stands(b, ("query", h, 0)):
                            pe.wait_ge(bank_emptied, turn)
                        pe.wait_ge(emptied[bank_no(*part, 0)], free(b, *part, 0))
                        bank = bank_of(*part, 0)
                        for t in range(TILES):
                            for half in range(2):
                                last = pe.matmul(bank[:, (t * 2 + half) * P:(t * 2 + half + 1) * P],
                                                 queryT[:, half, t * P:t * P + P], keys[:, half, :],
                                                 start=True, stop=True)
                        last.then_inc(bank_full, 1)
                    yield

            def up(b, g):
                t, s0 = g // TGROUPS, (g % TGROUPS) * PAIR
                if g == TGROUPS:
                    pe.wait_ge(acc_read, at(b, TILES, 1))
                pe.wait_ge(diag_ready, at(b, GROUPS, g + 1))
                for i in range(PAIR):
                    buf = buffer(g, i)
                    for n in range(2):
                        last = pe.matmul(acc[:, n * 512:n * 512 + 512], diag[:, g % 2, i, :],
                                         rows[:, buf, 1, n * 512:n * 512 + 512],
                                         start=s0 + i == 0, stop=s0 + i == SLOTS - 1, skip_group_check=True)
                last.then_inc(up_done, 1)

            def peer(b, mix):
                done = [0]
                for g in range(GROUPS):
                    if mix:
                        spread(g, mix, done)
                    if g:
                        up(b, g - 1)
                up(b, GROUPS - 1)

            pe.wait_ge(const_landed, 48)
            for _ in mixer(0):
                pass
            with pe.Fori(0, BLOCKS - 1) as b:
                peer(b, mixer(b + 1))
            peer(BLOCKS - 1, None)

        @block.vector
        def _(dve):
            def mixer(b, parts=PARTS):
                chain = 0 if parts is PARTS else MIX_STEPS

                def count():
                    nonlocal chain
                    chain += 1
                    return at(b, MIX_STEPS + TAIL_STEPS, chain)

                def top16(vals, ids, src, scratch):
                    dve.max(vals[:, 0:8], src).then_inc(mix_step, 1)
                    dve.wait_ge(mix_step, count())
                    settle(dve)
                    dve.max_index(ids[:, 0:8], vals[:, 0:8], src)
                    dve.match_replace(scratch, vals[:, 0:8], src, LOWEST).then_inc(mix_step, 1)
                    dve.wait_ge(mix_step, count())
                    settle(dve)
                    dve.max(vals[:, 8:16], scratch).then_inc(mix_step, 1)
                    dve.wait_ge(mix_step, count())
                    settle(dve)
                    return dve.max_index(ids[:, 8:16], vals[:, 8:16], scratch)

                for part in parts:
                    kind, *pos = part
                    first = isinstance(b, int) and b == 0
                    if kind == "kv":
                        dve.wait_ge(bank_full, filled(b, *part, 0))
                        bank = bank_of(*part, 0)
                        dve.tensor_copy(kT[:, 0, :], kT[:, 2, :])
                        dve.tensor_copy(v[:, 0, :], v[:, 2, :]).then_inc(mix_step, 1)
                        dve.wait_ge(mix_step, count())
                        dve.tensor_copy(kT[:, 1:3, :].rearrange("p a n -> p (a n)"), bank[:, 0:NT])
                        dve.tensor_copy(v[:, 1:3, :].rearrange("p a n -> p (a n)"), bank[:, NT:]).then_inc(emptied[bank_no(*part, 0)], 1)
                    elif kind == "scores":
                        c, h = pos
                        lo = P if first and c == 0 else 0
                        for i in range(2):
                            dve.wait_ge(bank_full, filled(b, *part, i))
                            bank = bank_of(*part, i)
                            for j in range(2):
                                ins = dve.scalar_tensor_tensor(
                                    out=probs[:, 2 * i + j, lo:], in0=dist[:, lo:], scalar=-slopes[h * GROUP + 2 * i + j],
                                    in1=bank[:, j * NT + lo:(j + 1) * NT], op0=ALU.mult, op1=ALU.add)
                            ins.then_inc(emptied[bank_no(*part, i)], 1)
                        for bank_emptied, turn in stands(b, (*part, 0), (*part, 1)):
                            dve.wait_ge(bank_emptied, turn)
                        dve.tensor_reduce(small[:, 0:4], probs[:, :, lo:], AX, ALU.max).then_inc(mix_step, 1)
                        dve.wait_ge(mix_step, count())
                        sinks = par[:, R_SINK + h * GROUP:R_SINK + (h + 1) * GROUP]
                        dve.tensor_tensor(small[:, 0:4], small[:, 0:4], sinks, ALU.max).then_inc(mix_step, 1)
                        dve.wait_ge(mix_step, count())
                        dve.tensor_scalar(small[:, 4:8], small[:, 0:4], -1.0, None, ALU.mult)
                        dve.tensor_tensor(small[:, 8:12], sinks, small[:, 0:4], ALU.subtract).then_inc(max_ready, 1)
                        dve.wait_ge(exp_done, at(b, 2 * KVH, c * KVH + h + 1))
                        dve.tensor_tensor(small[:, 20:24], small[:, 12:16], small[:, 16:20], ALU.add).then_inc(mix_step, 1)
                        dve.wait_ge(mix_step, count())
                        dve.reciprocal(small[:, 24:28], small[:, 20:24]).then_inc(mix_step, 1)
                        dve.wait_ge(mix_step, count())
                        for j in range(GROUP):
                            ins = dve.tensor_scalar(probs[:, j, lo:], probs[:, j, lo:], small[:, 24 + j:25 + j], None,
                                                    ALU.mult)
                        ins.then_inc(probs_ready, 1)
                    elif kind == "vr":
                        i = pos[0]
                        dve.wait_ge(bank_full, filled(b, *part, 0))
                        bank = bank_of(*part, 0)
                        dve.tensor_copy(vr[:, :, i * NT:i * NT + NT],
                                              bank.rearrange("p (t n) -> p t n", t=TILES)).then_inc(emptied[bank_no(*part, 0)], 1)
                    elif kind == "gr":
                        i = pos[0]
                        dve.wait_ge(bank_full, filled(b, *part, 0))
                        bank = bank_of(*part, 0)
                        e = gates[:, i % 2].rearrange("p a n -> p (a n)")
                        dve.wait_ge(swish_exp, at(b, 2, i + 1))
                        dve.tensor_scalar(e, e, 1.0, None, ALU.add).then_inc(mix_step, 1)
                        dve.wait_ge(mix_step, count())
                        dve.reciprocal(e, e).then_inc(mix_step, 1)
                        dve.wait_ge(mix_step, count())
                        dve.tensor_tensor(
                            swish[:, :, i * NT:i * NT + NT], bank.rearrange("p (t n) -> p t n", t=TILES),
                            e.rearrange("p (t n) -> p t n", t=TILES), ALU.mult).then_inc(mix_step, 1)
                        dve.wait_ge(mix_step, count())
                        gain = par[:, R_GN + i * NT:R_GN + i * NT + NT].unsqueeze(1).to_broadcast([P, TILES, NT])
                        dve.tensor_tensor(swish[:, :, i * NT:i * NT + NT], swish[:, :, i * NT:i * NT + NT],
                                                gain, ALU.mult).then_inc(emptied[bank_no(*part, 0)], 1)
                    elif kind == "gate":
                        m = pos[0]
                        for bank_emptied, turn in stands(b, (*part, 0)):
                            dve.wait_ge(bank_emptied, turn)
                        e = gates[:, m % 2].rearrange("p a n -> p (a n)")
                        dve.tensor_scalar(e, e, 1.0, None, ALU.add).then_inc(mix_step, 1)
                        dve.wait_ge(mix_step, count())
                        dve.reciprocal(e, e).then_inc(mix_step, 1)
                        dve.wait_ge(mix_step, count())
                    elif kind == "ret_scores":
                        c = pos[0]
                        dve.wait_ge(bank_full, filled(b, *part, 0))
                        bank = bank_of(*part, 0)
                        dve.tensor_tensor(maskedT[:, :], bank, rmask, ALU.mult).then_inc(emptied[bank_no(*part, 0)], 1)
                        dve.wait_ge(bank_full, filled(b, *part, 1))
                        bank = bank_of(*part, 1)
                        dve.tensor_tensor(kd[:, :].rearrange("p (h n) -> p h n", h=RH),
                                                bank.rearrange("p (h n) -> p h n", h=RH),
                                                kdec.unsqueeze(2).to_broadcast([P, RH, P]), ALU.mult).then_inc(emptied[bank_no(*part, 1)], 1)
                        for bank_emptied, turn in stands(b, ("qr", 0, 0), ("qr", 1, 0)):
                            dve.wait_ge(bank_emptied, turn)
                        dve.tensor_tensor(qd[:, :, :], qrT[:, :, c * P:c * P + P], qdec, ALU.mult).then_inc(qd_ready, 1)
                    elif kind == "ret_out":
                        c = pos[0]
                        dve.wait_ge(bank_full, filled(b, *part, 0))
                        bank = bank_of(*part, 0)
                        for h in range(RH):
                            ins = dve.bn_stats(stats[:, h, :], bank[:, h * P:h * P + P])
                        ins.then_inc(mix_step, 1)
                        dve.wait_ge(mix_step, count())
                        settle(dve)
                        for h in range(RH):
                            ins = dve.bn_aggr(mv[:, h, :], stats[:, h, :])
                        ins.then_inc(mix_step, 1)
                        dve.wait_ge(mix_step, count())
                        dve.tensor_copy(variance[:, :], mv[:, :, 1]).then_inc(mix_step, 1)
                        dve.wait_ge(mix_step, count())
                        inverse_root(mix_step, count, rstd[:, :], variance[:, :], roottmp[:, :])
                        for h in range(RH):
                            ins = dve.tensor_scalar(ret[:, h * P:h * P + P], bank[:, h * P:h * P + P], mv[:, h, 0:1],
                                                    rstd[:, h:h + 1], ALU.subtract, ALU.mult)
                        ins.then_inc(emptied[bank_no(*part, 0)], 1)
                        for bank_emptied, turn in stands(b, (*part, 0), ("gr", 0, 0), ("gr", 1, 0)):
                            dve.wait_ge(bank_emptied, turn)
                        dve.tensor_tensor(ret[:, :], ret[:, :], swish[:, c, :], ALU.mult).then_inc(ret_ready, 1)
                        dve.wait_ge(bank_full, filled(b, *part, 1))
                        bank = bank_of(*part, 1)
                        for h in range(RH):
                            o = slice(h * P, h * P + P)
                            ins = dve.scalar_tensor_tensor(out=state[:, o], in0=state[:, o], scalar=chunk_decay[h],
                                                           in1=bank[:, o], op0=ALU.mult, op1=ALU.add)
                        ins.then_inc(emptied[bank_no(*part, 1)], 1)
                    elif kind == "branch":
                        m = pos[0]
                        dve.wait_ge(bank_full, filled(b, *part, 0))
                        bank = bank_of(*part, 0)
                        g = gates[:, m % 2].rearrange("p a n -> p (a n)")
                        dve.tensor_tensor(g, g, bank, ALU.mult).then_inc(mix_step, 1)
                        dve.wait_ge(mix_step, count())
                        ins = dve.tensor_tensor(merged[:, m, :], g[:, 0:NT], g[:, NT:], ALU.add)
                        ins.then_inc(emptied[bank_no(*part, 0)], 1)
                    elif kind == "out":
                        n = pos[0]
                        if n == 0:
                            dve.wait_ge(xn_landed, at(b, 16, 16))
                        dve.wait_ge(bank_full, filled(b, *part, 0))
                        bank = bank_of(*part, 0)
                        to = x1n[:, :, n * NT:n * NT + NT]
                        dve.scalar_tensor_tensor(out=to, in0=to, scalar=ALPHA,
                                                       in1=bank.rearrange("p (t n) -> p t n", t=TILES),
                                                       op0=ALU.mult, op1=ALU.add).then_inc(emptied[bank_no(*part, 0)], 1)
                    elif kind == "norm":
                        t = pos[0]
                        for bank_emptied, turn in stands(b, *(("out", n, 0) for n in range(4))):
                            dve.wait_ge(bank_emptied, turn)
                        for i in range(2):
                            ins = dve.bn_stats(stats[:, i, :], x1n[:, t, i * 512:i * 512 + 512])
                        ins.then_inc(mix_step, 1)
                        dve.wait_ge(mix_step, count())
                        settle(dve)
                        dve.bn_aggr(mv[:, 0, :], stats[:, 0:2, :].rearrange("p a s -> p (a s)")).then_inc(mix_step, 1)
                        dve.wait_ge(mix_step, count())
                        inverse_root(mix_step, count, rstd[:, 0:1], mv[:, 0, 1:2], roottmp[:, 0:1])
                        dve.tensor_scalar(x1n[:, t, :], x1n[:, t, :], mv[:, 0, 0:1], rstd[:, 0:1],
                                               ALU.subtract, ALU.mult).then_inc(mix_step, 1)
                        dve.wait_ge(mix_step, count())
                        dve.tensor_tensor(x1n[:, t, :], x1n[:, t, :], par[:, R_MG:R_MB], ALU.mult).then_inc(mix_step, 1)
                        dve.wait_ge(mix_step, count())
                        dve.tensor_tensor(x1n[:, t, :], x1n[:, t, :], par[:, R_MB:R_FG], ALU.add).then_inc(x1_ready, 1)
                    elif kind == "halves":
                        h = pos[0]
                        dve.wait_ge(bank_full, filled(b, *part, 0))
                        bank = bank_of(*part, 0)
                        settle(dve)
                        for t in range(TILES):
                            for half in range(2):
                                ins = top16(val[:, t, half, h, :], idx[:, t, half, h, :],
                                            bank[:, (t * 2 + half) * P:(t * 2 + half + 1) * P],
                                            rest[:, half, 0:P])
                        ins.then_inc(emptied[bank_no(*part, 0)], 1)
                    elif kind == "pick":
                        t, s = pos
                        if s == 0:
                            if t == 0:
                                for bank_emptied, turn in stands(b, ("halves", PH - 1, 0)):
                                    dve.wait_ge(bank_emptied, turn)
                            dve.tensor_tensor(
                                cand.rearrange("p h (i j) -> p h i j", i=TOPK),
                                val[:, t, 0].unsqueeze(3).to_broadcast([P, PH, TOPK, TOPK]),
                                val[:, t, 1].unsqueeze(2).to_broadcast([P, PH, TOPK, TOPK]), ALU.add).then_inc(mix_step, 1)
                            dve.wait_ge(mix_step, count())
                            dve.tensor_copy(idxf[:, :, :], idx[:, t].rearrange("p a h k -> p a (h k)")).then_inc(mix_step, 1)
                            dve.wait_ge(mix_step, count())
                            settle(dve)
                        elif s in (1, 2):
                            for h in range(PH // 2 * (s - 1), PH // 2 * s):
                                ins = top16(topv[:, h, :], topp[:, h * TOPK:(h + 1) * TOPK], cand[:, h, :],
                                            rest[:, h % 2, :])
                            ins.then_inc(mix_step, 1)
                            dve.wait_ge(mix_step, count())
                            if s == 1:
                                settle(dve)
                        elif s in (3, 4):
                            a = s - 3
                            dve.tensor_scalar(posu[:, a, :], topp[:, :], *((4, None, ALU.logical_shift_right)
                                                   if a == 0 else (TOPK - 1, None, ALU.bitwise_and))).then_inc(mix_step, 1)
                            dve.wait_ge(mix_step, count())
                            dve.tensor_copy(posf[:, a, :], posu[:, a, :]).then_inc(mix_step, 1)
                            dve.wait_ge(mix_step, count())
                            dve.tensor_tensor(onehot, posf[:, a, :].unsqueeze(2).to_broadcast([P, SLOTS, TOPK]),
                                                   iota.unsqueeze(1).to_broadcast([P, SLOTS, TOPK]), ALU.is_equal).then_inc(mix_step, 1)
                            dve.wait_ge(mix_step, count())
                            hot = onehot.rearrange("p (h s) a -> p h s a", h=PH)
                            ids = idxf[:, a, :].rearrange("p (h a) -> p h a", h=PH)
                            dve.tensor_tensor(hot, hot, ids.unsqueeze(2).to_broadcast([P, PH, TOPK, TOPK]), ALU.mult).then_inc(mix_step, 1)
                            dve.wait_ge(mix_step, count())
                            dve.tensor_reduce(part_e[:, a, :], onehot, AX, ALU.add).then_inc(mix_step, 1)
                            dve.wait_ge(mix_step, count())
                        else:
                            dve.scalar_tensor_tensor(out=expert_next[:, t, :], in0=part_e[:, 0, :], scalar=float(NK),
                                                     in1=part_e[:, 1, :], op0=ALU.mult, op1=ALU.add)
                            dve.tensor_copy(gsum[:, 0, :], topv[:, :, 0]).then_inc(mix_step, 1)
                            dve.wait_ge(mix_step, count())
                            dve.tensor_tensor(topv[:, :, :], topv[:, :, :],
                                              gsum[:, 0, :].unsqueeze(2).to_broadcast([P, PH, TOPK]),
                                              ALU.subtract).then_inc(gdiff_ready, 1)
                            dve.wait_ge(gexp_done, at(b, TILES, t + 1))
                            dve.tensor_reduce(gsum[:, 0, :], topv[:, :, :], AX, ALU.add).then_inc(mix_step, 1)
                            dve.wait_ge(mix_step, count())
                            dve.reciprocal(gsum[:, 1, :], gsum[:, 0, :]).then_inc(mix_step, 1)
                            dve.wait_ge(mix_step, count())
                            dve.tensor_tensor(gate_next[:, t, :].rearrange("p (h k) -> p h k", h=PH), topv[:, :, :],
                                                   gsum[:, 1, :].unsqueeze(2).to_broadcast([P, PH, TOPK]), ALU.mult).then_inc(mix_step, 1)
                            dve.wait_ge(mix_step, count())
                    elif kind == "publish":
                        publish(0)
                    if part == parts[-1]:
                        assert chain == (MIX_STEPS if parts is PARTS else MIX_STEPS + TAIL_STEPS), chain
                    yield

            def inverse_root(step, count, out, var, tmp):
                dve.tensor_scalar(var, var, EPS, None, ALU.add).then_inc(step, 1)
                dve.wait_ge(step, count())
                dve.tensor_scalar(tmp.bitcast(U32), var.bitcast(U32), 1, None, ALU.logical_shift_right).then_inc(step, 1)
                dve.wait_ge(step, count())
                dve.tensor_scalar(out.bitcast(U32), tmp.bitcast(U32), -1.0, float(0x5F3759DF), ALU.mult, ALU.add).then_inc(step, 1)
                dve.wait_ge(step, count())
                for _ in range(3):
                    dve.scalar_tensor_tensor(out=tmp, in0=out, scalar=-0.5, in1=out, op0=ALU.mult, op1=ALU.mult).then_inc(step, 1)
                    dve.wait_ge(step, count())
                    dve.tensor_tensor(tmp, tmp, var, ALU.mult).then_inc(step, 1)
                    dve.wait_ge(step, count())
                    dve.scalar_tensor_tensor(out=out, in0=tmp, scalar=1.5, in1=out, op0=ALU.add, op1=ALU.mult).then_inc(step, 1)
                    dve.wait_ge(step, count())

            def publish(t):
                dve.tensor_copy(gate[:, t, :], gate_next[:, t, :])
                dve.tensor_copy(x1[:, t, :], x1n[:, t, :])
                dve.tensor_copy(expert[:, t, :], expert_next[:, t, :]).then_inc(published, 1)

            def finish(b, t):
                n = 0

                def count():
                    nonlocal n
                    n += 1
                    return at(b, FIN_STEPS * TILES, FIN_STEPS * t + n)

                dve.wait_ge(up_done, at(b, GROUPS, TGROUPS * (t + 1)))
                dve.wait_ge(stored, at(b, 16 * TILES, 16 * (t + 1)))
                dve.scalar_tensor_tensor(out=y[:, :], in0=x1[:, t, :], scalar=ALPHA, in1=acc,
                                         op0=ALU.mult, op1=ALU.add).then_inc(acc_read, 1)
                dve.wait_ge(acc_read, at(b, TILES, t + 1))
                for i in range(2):
                    ins = dve.bn_stats(fstats[:, i, :], y[:, i * 512:i * 512 + 512])
                ins.then_inc(fin_step, 1)
                dve.wait_ge(fin_step, count())
                settle(dve)
                dve.bn_aggr(fmv[:, :], fstats[:, :, :].rearrange("p a s -> p (a s)")).then_inc(fin_step, 1)
                dve.wait_ge(fin_step, count())
                inverse_root(fin_step, count, frstd[:, :], fmv[:, 1:2], roottmp[:, 0:1])
                dve.tensor_scalar(y[:, :], y[:, :], fmv[:, 0:1], frstd[:, 0:1], ALU.subtract, ALU.mult).then_inc(fin_step, 1)
                dve.wait_ge(fin_step, count())
                dve.tensor_tensor(y[:, :], y[:, :], par[:, R_FG:R_FB], ALU.mult).then_inc(fin_step, 1)
                dve.wait_ge(fin_step, count())
                dve.tensor_tensor(y[:, :], y[:, :], par[:, R_FB:R_GN], ALU.add).then_inc(out_ready, 1)
                assert n == FIN_STEPS

            MIX_STEPS, TAIL_STEPS, FIN_STEPS = 247, 42, 16

            def dots(b, g):
                t = g // TGROUPS
                for i in range(PAIR):
                    buf = buffer(g, i)
                    dve.wait_ge(gathered[buf], arrived(b, g))
                    ins = dve.tensor_tensor_reduce(rows[:, buf, 0, :], rows[:, buf, 0, :], x1[:, t, :], 1.0, 0.0,
                                                   ALU.mult, ALU.add, hdot[:, g % 2, i:i + 1])
                ins.then_inc(dots_done, 1)

            def diagonals(b, g):
                t, s0 = g // TGROUPS, (g % TGROUPS) * PAIR
                dve.wait_ge(gelu_done, at(b, GROUPS, g + 1))
                if g > 1:
                    dve.wait_ge(up_done, at(b, GROUPS, g - 1))
                for i in range(PAIR):
                    ins = dve.tensor_scalar(diag[:, g % 2, i, :], ident, hact[:, g % 2, i:i + 1],
                                            gate[:, t, s0 + i:s0 + i + 1], ALU.mult, ALU.mult)
                ins.then_inc(diag_ready, 1)

            def peer(b, mix):
                done = [0]
                tail = mixer(b, TAIL)
                for g in range(GROUPS):
                    dots(b, g)
                    if g:
                        diagonals(b, g - 1)
                    if g < len(TAIL):
                        next(tail)
                    elif g == len(TAIL):
                        publish(1)
                    if mix:
                        spread(g - 1, mix, done)
                    if g == TGROUPS + 1:
                        finish(b, 0)
                diagonals(b, GROUPS - 1)
                finish(b, 1)

            dve.wait_ge(const_landed, 48)
            for bank in range(BANKS):
                dve.sem_inc(emptied[bank], 1)
            dve.memset(small[:, :], 0.0)
            dve.memset(probs[:, :, :], 0.0)
            dve.memset(kT[:, 2, :], 0.0)
            dve.memset(v[:, 2, :], 0.0)
            dve.memset(state[:, :], 0.0).then_inc(state_zeroed, 1)
            dve.wait_ge(state_zeroed, 1)
            for _ in mixer(0):
                pass
            with dve.Fori(0, BLOCKS - 1) as b:
                peer(b, mixer(b + 1))
            peer(BLOCKS - 1, None)


def kernel(**inputs):
    import numpy as _np
    import concourse.bacc as _bacc
    from concourse import mybir as _mybir
    from concourse.bass_utils import run_bass_kernel_spmd as _run

    a = {k: _np.asarray(v) for k, v in inputs.items()}
    x = a["x"][0]
    splits = _np.cumsum([0, AH * HD, KVH * HD, KVH * HD, RH * P, RH * P, RH * P, RH * P, D, D])
    qa, ka, va, qr, kr, vr, gr, ga, gb = (a["w_in"][0][:, splits[i]:splits[i + 1]] for i in range(9))

    def unit(w):
        return w.reshape(-1, P, P).transpose(1, 0, 2)

    heads = _np.concatenate([_np.r_[j * HD:(j + 1) * HD, (j + GROUP) * HD:(j + GROUP + 1) * HD] for j in range(GROUP)])
    qa = qa[:, heads]
    wa, wr = a["w_attn_branch"][0][heads], a["w_ret_branch"][0]
    wo, wq = a["w_out"][0], a["w_peer_query"][0]

    def col(w, n):
        return unit(w[:, n * P:(n + 1) * P])

    def pair(p):
        kind, i = p[0], p[1] if len(p) > 1 else 0
        if kind == "kv":
            return col(ka, 0), col(va, 0)
        if kind == "gate":
            return col(ga, i), col(gb, i)
        if kind == "branch":
            return tuple(_np.concatenate([col(wa, m), col(wr, m)], axis=1) for m in (i, i + 1))
        w = {"qa": qa, "qr": qr, "kr": kr, "vr": vr, "gr": gr, "out": wo, "query": wq}[kind]
        return col(w, 2 * i), col(w, 2 * i + 1)

    weights = _np.stack([_np.stack(pair(p), axis=1).reshape(P, 2 * D) for p in PAIRS])
    par = _np.concatenate([a[n][0] for n in ("ln_mix_gain", "ln_mix_bias", "ln_ffn_gain", "ln_ffn_bias",
                                             "ret_gn_gain", "attn_sinks")])
    arrays = {
        "xT_dram": x.T.reshape(KD, P, BLOCKS, NT).transpose(2, 1, 0, 3),
        "xn_dram": x.reshape(BLOCKS, TILES, P, D).transpose(0, 2, 1, 3),
        "weights_dram": weights,
        "keys_dram": a["peer_sub_keys"][0].transpose(2, 0, 1),
        "const_dram": constants(),
        "par_dram": _np.broadcast_to(par, (P, len(par))),
        "rows_dram": _np.concatenate([a["peer_down"][0], a["peer_up"][0]], axis=1),
    }
    arrays = {k: _np.ascontiguousarray(v) for k, v in arrays.items()}
    nc = _bacc.Bacc("TRN2", target_bir_lowering=False, num_devices=1)
    args = [nc.dram_tensor(k, v.shape, _mybir.dt.from_np(v.dtype), kind="ExternalInput").ap()
            for k, v in arrays.items()]
    out = nc.dram_tensor("out_dram", (BLOCKS, TILES, P, D), F32, kind="ExternalOutput").ap()
    build(nc, *args, out)
    r = _run(nc, [arrays], core_ids=[0])
    return r.results[0]["out_dram"].reshape(1, S, D)
```

```python
from contextlib import ExitStack

import concourse.bass as bass
import numpy as np
from concourse import mybir

F32 = mybir.dt.float32
U32 = mybir.dt.uint32
ALU = mybir.AluOpType
ACT = mybir.ActivationFunctionType
AX = mybir.AxisListType.X

P = 128
D = 1024
KD = D // P
S = 1024
TILES = 2
NT = TILES * P
BLOCKS = S // NT
HD, KVH, GROUP = 64, 2, 4
AH = KVH * GROUP
RH = 4
PH, TOPK, NK = 8, 16, 128
SLOTS = PH * TOPK
ALPHA = float(2.0 ** 0.25)
EPS = 1e-5
FAR = 1.0e30
LOWEST = -3.0e38

RING = 10
PAIR = 2
GROUPS = TILES * SLOTS // PAIR
TGROUPS = SLOTS // PAIR
_ROUNDS = -(-GROUPS // (RING // PAIR))
_SHORT = _ROUNDS * (RING // PAIR) - GROUPS
PLACE = [j for r in range(_ROUNDS) for j in range(RING // PAIR - ((r + 1) * _SHORT // _ROUNDS > r * _SHORT // _ROUNDS))]
WRING = 3
BANKS = 4

PICKS = [("rows", 0), ("rows", 1), ("columns", 0), ("columns", 1), ("softmax", 0)]
PARTS = (
    [("kv",), ("qa", 0), ("qa", 1), ("scores", 0, 0), ("qr", 0), ("turn", 0, 0), ("scores", 0, 1),
     ("qr", 1), ("pv", 0, 0), ("turn", 0, 1), ("scores", 1, 0), ("kr", 0), ("pv", 0, 1), ("turn", 1, 0),
     ("scores", 1, 1), ("kr", 1), ("pv", 1, 0), ("turn", 1, 1), ("vr", 0), ("pv", 1, 1), ("vr", 1),
     ("gr", 0), ("ret_scores", 0), ("gr", 1), ("ret_out", 0), ("gate", 0), ("ret_turn", 0),
     ("ret_scores", 1), ("gate", 1), ("ret_out", 1), ("ret_turn", 1)]
    + [p for m in range(0, KD, 2)
       for p in ([("gate", m), ("gate", m + 1)] if m else []) + [("branch", m), ("branch", m + 1)]]
    + [("out", n) for n in range(4)] + [("norm", 0), ("norm", 1), ("x1turn", 0), ("x1turn", 1)]
    + [p for h in range(PH) for p in (("query", h), ("halves", h))]
    + [("pick", 0, *s) for s in PICKS] + [("publish",)]
)
TAIL = tuple([("rank", h) for h in range(PH)] + [("pick", 1, *s) for s in PICKS])
HEAD = 5
TAIL_AT = [HEAD + 2 * h for h in range(PH)] + [HEAD + 2 * PH + n for n in range(len(PICKS))]
TAIL_END = TAIL_AT[-1] + 1
AHEAD = 3
MIX_END = GROUPS - 7
_LONG = ("halves", "kv", "qa", "qr", "kr", "vr", "gr", "gate", "out", "query", "scores", "ret_out", "norm")
EFFORT = np.cumsum([4 if p[0] in _LONG or p[0] == "pick" else 2 for p in PARTS]).tolist()
PAIRS = [p for p in PARTS if p[0] in ("kv", "qa", "qr", "kr", "vr", "gr", "gate", "out", "query")
         or (p[0] == "branch" and p[1] % 2 == 0)]
PAIR_AT = {p: n for n, p in enumerate(PAIRS)}
for _m in range(1, KD, 2):
    PAIR_AT[("branch", _m)] = PAIR_AT[("branch", _m - 1)]
USES = []
for _p in PARTS:
    _n = {"scores": 2, "turn": 2, "ret_scores": 2, "ret_out": 2, "x1turn": 2, "norm": 0, "rank": 0, "pick": 0, "publish": 0}
    USES += [(*_p, i) for i in range(_n.get(_p[0], 1))]
USE_AT = {u: n for n, u in enumerate(USES)}
LAST_USE = [USE_AT[(p[0], p[1] + 1, 0) if p[0] == "branch" else (*p, 0)] for p in PAIRS]
BANK_USES = [len(range(b, len(USES), BANKS)) for b in range(BANKS)]
BUF_PAIRS = [len(range(b, len(PAIRS), WRING)) for b in range(WRING)]

C_IDENT, C_DIST, C_RMASK, C_QDEC, C_KDEC, C_IOTA, C_END = np.cumsum([0, P, 2 * P, RH * P, RH * P, RH, TOPK]).tolist()
R_MG, R_MB, R_FG, R_FB, R_GN, R_SINK, R_END = np.cumsum([0, D, D, D, D, RH * P, AH]).tolist()


def log_gammas():
    return np.log1p(-(2.0 ** (-5.0 - np.arange(RH, dtype=np.float32)))).astype(np.float32)


def constants():
    c = np.zeros((P, C_END), np.float32)
    c[:, C_IDENT:C_DIST] = np.eye(P)
    dist = (np.arange(P)[:, None] + P) - np.arange(2 * P)[None, :]
    c[:, C_DIST:C_RMASK] = np.where((dist >= 0) & (dist < P), dist, FAR)
    lg = log_gammas()
    pos = np.arange(P, dtype=np.float32)
    for h in range(RH):
        diff = pos[None, :] - pos[:, None]
        c[:, C_RMASK + h * P:C_RMASK + (h + 1) * P] = np.where(diff >= 0, np.exp(np.maximum(diff, 0) * lg[h]), 0)
        c[:, C_QDEC + h * P:C_QDEC + (h + 1) * P] = np.exp((pos + 1) * lg[h])[None, :]
        c[:, C_KDEC + h] = np.exp((P - 1 - pos) * lg[h])
    c[:, C_IOTA:C_END] = np.arange(TOPK)[None, :]
    return c


def build(nc, xT_d, xn_d, w_d, keys_d, const_d, par_d, rows_d, out_d):
    slopes = [float(2.0 ** (-8.0 * (h + 1) / AH)) for h in range(AH)]
    chunk_decay = [float(np.exp(np.float32(P) * g)) for g in log_gammas()]
    with ExitStack() as ctx:
        def sb(name, shape, dt=F32):
            return ctx.enter_context(nc.sbuf_tensor(name, shape, dt))

        def sem(name):
            return ctx.enter_context(nc.semaphore(name))

        ps = ctx.enter_context(nc.psum_tensor("ps", [P, 8, 512], F32))
        acc = ps[:, BANKS:8, :].rearrange("p (t a) b -> p t (a b)", t=TILES)

        const = sb("const", [P, C_END])
        ident = const[:, C_IDENT:C_DIST]
        dist = const[:, C_DIST:C_RMASK]
        rmask = const[:, C_RMASK:C_QDEC]
        qdec = const[:, C_QDEC:C_KDEC].rearrange("p (h i) -> p h i", h=RH)
        kdec = const[:, C_KDEC:C_IOTA]
        iota = const[:, C_IOTA:C_END]
        par = sb("par", [P, R_END])
        keys = sb("keys", [P, 2, NK])
        weights = sb("weights", [P, WRING, 2, KD, P])
        rows = sb("rows", [P, RING, 2, D])
        xT = sb("xT", [P, KD, NT])
        x1n = sb("x1n", [P, TILES, D])
        qrT = x1n[:, 0, :].rearrange("p (h n) -> p h n", h=RH)
        krT = x1n[:, 1, :].rearrange("p (h n) -> p h n", h=RH)
        kT = sb("kT", [P, 3, P])
        v = sb("v", [P, 3, P])
        vr = sb("vr", [P, TILES, RH * P])
        gates = sb("gates", [P, 2, 2, NT])
        pick8k = sb("pick8k", [P, 2, D])
        probs = pick8k[:, 0, :].rearrange("p (j s) -> p j s", j=GROUP)
        probsT = pick8k[:, 1, :].rearrange("p (k n) -> p k n", k=2)
        cand = pick8k[:, 0, 0:2 * TOPK * TOPK].rearrange("p (h c) -> p h c", h=2)
        attnT = sb("attnT", [P, GROUP, NT])
        retT = pick8k[:, 1, :].rearrange("p (h n) -> p h n", h=RH)
        maskedT = sb("maskedT", [P, RH * P])
        kd = sb("kd", [P, RH * P])
        qd = sb("qd", [P, RH, P])
        ret = sb("ret", [P, RH * P])
        state = sb("state", [P, RH * P])
        merged = sb("merged", [P, KD, NT])
        qT = merged[:, 0:GROUP, :]
        swish = merged[:, GROUP:, :].rearrange("p a b -> p (a b)").rearrange("p (t n) -> p t n", t=TILES)
        kept = merged[:, :, :].rearrange("p a b -> p (a b)").rearrange("p (h a n) -> p h a n", h=PH, a=2)
        onehot = gates[:, :, :, :].rearrange("p a b n -> p (a b n)").rearrange("p (s a) -> p s a", a=TOPK)
        queryT = attnT[:, 0:2, :]
        small = sb("small", [P, 32])
        stats = sb("stats", [P, RH, 6])
        mv = sb("mv", [P, RH, 2])
        rstd = sb("rstd", [P, RH])
        variance = sb("variance", [P, RH])
        roottmp = sb("roottmp", [P, RH])
        rest = vr[:, 0, :].rearrange("p (a c) -> p a c", a=2)
        val = maskedT[:, :].rearrange("p (t a h k) -> p t a h k", t=TILES, a=2, h=PH)
        idx = kd[:, :].bitcast(U32).rearrange("p (t a h k) -> p t a h k", t=TILES, a=2, h=PH)
        idxf, posf = (qd[:, 2 * i:2 * i + 2, :] for i in range(2))
        part_e = ret[:, 0:2 * SLOTS].rearrange("p (a s) -> p a s", a=2)
        posu = ret[:, 2 * SLOTS:].bitcast(U32).rearrange("p (a s) -> p a s", a=2)
        topv = sb("topv", [P, PH, TOPK])
        topp = sb("topp", [P, SLOTS], U32)
        gsum = sb("gsum", [P, 2, PH])
        expert_next = sb("expert_next", [P, TILES, SLOTS], U32)
        gate_next = sb("gate_next", [P, TILES, SLOTS])
        expert = sb("expert", [P, TILES, SLOTS], U32)
        gate = sb("gate", [P, TILES, SLOTS])
        x1 = sb("x1", [P, TILES, D])
        hdot = sb("hdot", [P, 2, PAIR])
        hact = sb("hact", [P, 2, PAIR])
        diag = sb("diag", [P, 2, PAIR, P])
        y = sb("y", [P, D])
        fstats = sb("fstats", [P, 2, 6])
        fmv = sb("fmv", [P, 2])
        frstd = sb("frstd", [P, 1])

        const_landed, par_landed, keys_landed = sem("const_landed"), sem("par_landed"), sem("keys_landed")
        landed = [sem(f"weights_landed{b}") for b in range(WRING)]
        xT_landed, xn_landed = sem("xT_landed"), sem("xn_landed")
        bank_full = sem("bank_full")
        emptied = [sem(f"bank_emptied{b}") for b in range(BANKS)]
        state_zeroed = sem("state_zeroed")
        max_ready, exp_done, probs_ready = sem("max_ready"), sem("exp_done"), sem("probs_ready")
        scores_kept = sem("scores_kept")
        qd_ready, ret_ready, x1_ready = sem("qd_ready"), sem("ret_ready"), sem("x1_ready")
        gdiff_ready, gexp_done = sem("gdiff_ready"), sem("gate_exp_done")
        swish_exp = sem("swish_exp")
        mix_step, fin_step = sem("mix_step"), sem("fin_step")
        published = sem("published")
        gathered = [sem(f"gathered{b}") for b in range(RING)]
        dots_done, gelu_done, diag_ready = sem("dots_done"), sem("gelu_done"), sem("diag_ready")
        up_done, acc_read = sem("up_done"), sem("acc_read")
        out_ready, stored = sem("out_ready"), sem("stored")
        passed = [sem("vector_passed"), sem("pool_passed")]
        pool_engine = nc.gpsimd

        def at(b, per, n):
            return b * per + n

        def started(b):
            return not isinstance(b, int) or b > 0

        def filled(b, *use):
            return at(b, len(USES), USE_AT[use] + 1)

        def bank_no(*use):
            return USE_AT[use] % BANKS

        def bank_of(*use):
            return ps[:, bank_no(*use), :]

        def free(b, *use):
            return at(b, BANK_USES[bank_no(*use)], USE_AT[use] // BANKS + 1)

        def stands(b, *uses, before=None):
            last = {bank_no(*u): u for u in sorted(uses, key=USE_AT.get)}
            return [(emptied[n], free(b, *u) + 1) for n, u in last.items() if before is None or n != bank_no(*before)]

        def buffer(g, i):
            return PLACE[g] * PAIR + i

        def arrived(b, g):
            return at(b, 16 * PLACE.count(PLACE[g]), 16 * PLACE[:g + 1].count(PLACE[g]))

        def used_before(b, g):
            n = max([m for m in range(g) if PLACE[m] == PLACE[g]], default=None)
            if n is None:
                return at(b, GROUPS, max(m for m in range(GROUPS) if PLACE[m] == PLACE[g]) + 1 - GROUPS) if started(b) else None
            return at(b, GROUPS, n + 1)

        def settle(eng):
            eng.sem_inc(passed[eng is pool_engine], 1)

        def spread(g, mix, done, ahead=False):
            share = EFFORT[-1] * (g - TAIL_END + 1) / (MIX_END - TAIL_END)
            goal = sum(effort <= share for effort in EFFORT)
            if ahead:
                goal = max(goal, min(AHEAD, g - TAIL_END + AHEAD + 1))
            while done[0] < goal:
                next(mix)
                done[0] += 1

        block = ctx.enter_context(nc.Block())

        @block.sync
        def _(sp):
            def loads(b):
                if started(b):
                    sp.wait_ge(bank_full, at(b, len(USES), 0))
                sp.dma_start(xT[:, :, :], xT_d[bass.ds(b, 1)].rearrange("b p k n -> (b p) k n")).then_inc(xT_landed, 16)
                for n, pair in enumerate(PAIRS):
                    if n >= WRING:
                        sp.wait_ge(bank_full, at(b, len(USES), LAST_USE[n - WRING] + 1))
                    elif started(b):
                        last = max(m for m in range(len(PAIRS)) if m % WRING == n)
                        sp.wait_ge(bank_full, at(b - 1, len(USES), LAST_USE[last] + 1))
                    sp.dma_start(weights[:, n % WRING].rearrange("p u k c -> p (u k c)"),
                                 w_d[n]).then_inc(landed[n % WRING], 16)
                    if isinstance(b, int) and n == 0:
                        sp.dma_start(const[:, :], const_d).then_inc(const_landed, 16)
                    if isinstance(b, int) and n == WRING - 1:
                        sp.dma_start(par[:, :], par_d).then_inc(par_landed, 16)
                        sp.dma_start(keys[:, :, :], keys_d).then_inc(keys_landed, 16)
                    if pair == ("gate", 5):
                        sp.wait_ge(bank_full, filled(b, "ret_turn", 1, 0))
                        sp.dma_start(x1n[:, :, :],
                                     xn_d[bass.ds(b, 1)].rearrange("b p t d -> (b p) t d")).then_inc(xn_landed, 16)

            loads(0)
            with sp.Fori(1, BLOCKS) as b:
                loads(b)

        @block.gpsimd
        def _(pool):
            def gathers(b):
                for g in range(GROUPS):
                    t, s0 = g // TGROUPS, (g % TGROUPS) * PAIR
                    if g % TGROUPS == 0:
                        pool.wait_ge(published, at(b, TILES, t + 1))
                    if used_before(b, g) is not None:
                        pool.wait_ge(up_done, used_before(b, g))
                        settle(pool)
                    for i in range(PAIR):
                        buf = buffer(g, i)
                        pool.indirect_dma_start(
                            out=rows[:, buf].rearrange("p a d -> p (a d)"), out_offset=None, in_=rows_d,
                            in_offset=bass.IndirectOffsetOnAxis(ap=expert[:, t, s0 + i:s0 + i + 1], axis=0),
                        ).then_inc(gathered[buf], 16)

            gathers(0)
            with pool.Fori(1, BLOCKS) as b:
                gathers(b)

        @block.scalar
        def _(act):
            def copy(out, use, b, scale=1.0, part=None):
                act.wait_ge(bank_full, filled(b, *use))
                bank = bank_of(*use)
                act.activation(out, bank if part is None else bank[part], ACT.Copy, scale=scale).then_inc(emptied[bank_no(*use)], 1)

            def mixer(b, parts=PARTS):
                for part in parts:
                    kind, *pos = part
                    if kind == "qa":
                        i = pos[0]
                        if i == 0 and started(b):
                            act.wait_ge(published, at(b, TILES, 0))
                        copy(qT[:, 2 * i:2 * i + 2, :].rearrange("p j n -> p (j n)"), (*part, 0), b, HD ** -0.5)
                    elif kind in ("qr", "kr"):
                        i = pos[0]
                        to = qrT if kind == "qr" else krT
                        copy(to[:, 2 * i:2 * i + 2, :].rearrange("p j n -> p (j n)"), (*part, 0), b,
                             P ** -0.5 if kind == "qr" else 1.0)
                    elif kind == "scores":
                        c, h = pos
                        n = c * KVH + h
                        lo = P if isinstance(b, int) and b == 0 and c == 0 else 0
                        act.wait_ge(max_ready, at(b, 2 * KVH, n + 1))
                        for j in range(GROUP):
                            act.activation(probs[:, j, lo:], probs[:, j, lo:], ACT.Exp, bias=small[:, 4 + j:5 + j],
                                           accum_out=small[:, 12 + j:13 + j])
                        act.activation(small[:, 16:20], small[:, 8:12], ACT.Exp).then_inc(exp_done, 1)
                    elif kind == "turn":
                        c, h = pos
                        for k in range(2):
                            copy(probsT[:, k, :], (*part, k), b)
                    elif kind == "pv":
                        c, h = pos
                        half = slice(HD * h, HD * h + HD)
                        act.wait_ge(bank_full, filled(b, *part, 0))
                        bank = bank_of(*part, 0)
                        act.activation(attnT[half, :, c * P:c * P + P],
                                             bank[half].rearrange("p (j n) -> p j n", j=GROUP), ACT.Copy).then_inc(emptied[bank_no(*part, 0)], 1)
                    elif kind in ("gr", "gate"):
                        n = pos[0]
                        act.wait_ge(bank_full, filled(b, *part, 0))
                        bank = bank_of(*part, 0)
                        if kind == "gate":
                            for bank_emptied, turn in stands(b, ("branch", n - 2, 0) if n >= 2 else ("gr", n, 0)):
                                act.wait_ge(bank_emptied, turn)
                        elif started(b):
                            for bank_emptied, turn in stands(b - 1, ("branch", KD - 2 + n, 0)):
                                act.wait_ge(bank_emptied, turn)
                        ins = act.activation(gates[:, n % 2].rearrange("p a n -> p (a n)"), bank, ACT.Exp, scale=-1.0)
                        if kind == "gate":
                            ins.then_inc(emptied[bank_no(*part, 0)], 1)
                        else:
                            ins.then_inc(swish_exp, 1)
                    elif kind == "ret_turn":
                        c = pos[0]
                        act.wait_ge(bank_full, filled(b, *part, 0))
                        bank = bank_of(*part, 0)
                        act.activation(retT[:, :, c * P:c * P + P],
                                             bank.rearrange("p (h n) -> p h n", h=RH), ACT.Copy).then_inc(emptied[bank_no(*part, 0)], 1)
                    elif kind == "x1turn":
                        t = pos[0]
                        for i in range(2):
                            act.wait_ge(bank_full, filled(b, *part, i))
                            bank = bank_of(*part, i)
                            act.activation(xT[:, 4 * i:4 * i + 4, t * P:t * P + P],
                                                 bank.rearrange("p (k n) -> p k n", k=4), ACT.Copy).then_inc(emptied[bank_no(*part, i)], 1)
                    elif kind == "halves":
                        h = pos[0]
                        act.wait_ge(bank_full, filled(b, *part, 0))
                        bank = bank_of(*part, 0)
                        act.activation(kept[:, h].rearrange("p a n -> p (a n)"), bank[:, 2 * NK:], ACT.Copy).then_inc(scores_kept, 1)
                    elif kind == "query":
                        copy(queryT[:, :, :].rearrange("p a n -> p (a n)"), (*part, 0), b)
                    elif kind == "pick" and pos[1] == "softmax":
                        t = pos[0]
                        act.wait_ge(gdiff_ready, at(b, TILES, t + 1))
                        act.activation(topv[:, :, :], topv[:, :, :], ACT.Exp).then_inc(gexp_done, 1)
                    yield

            def gelu(b, g):
                act.wait_ge(dots_done, at(b, GROUPS, g + 1))
                if g > 1 or started(b):
                    act.wait_ge(diag_ready, at(b, GROUPS, g - 1))
                act.activation(hact[:, g % 2, :], hdot[:, g % 2, :], ACT.Gelu).then_inc(gelu_done, 1)

            def head(b):
                for g in range(HEAD):
                    gelu(b, g)
                if started(b):
                    store(b - 1, 1)

            def body(b, mix):
                done = [0]
                tail = mixer(b, TAIL)
                for g in range(HEAD, GROUPS):
                    gelu(b, g)
                    if g in TAIL_AT:
                        next(tail)
                    if mix:
                        spread(g - 1, mix, done)
                    if g == TGROUPS + 8:
                        store(b, 0)

            def store(b, t):
                act.wait_ge(out_ready, at(b, TILES, t + 1))
                act.dma_start(out_d[bass.ds(b, 1), t].rearrange("b p d -> (b p) d"), y[:, :]).then_inc(stored, 16)

            act.sem_inc(stored, 16)
            for _ in mixer(0):
                pass
            head(0)
            with act.Fori(0, BLOCKS - 1) as b:
                body(b, mixer(b + 1))
                head(b + 1)
            body(BLOCKS - 1, None)
            store(BLOCKS - 1, 1)
            act.wait_ge(stored, 16 * (TILES * BLOCKS + 1))

        @block.tensor
        def _(pe):
            def mixer(b, parts=PARTS):
                for part in parts:
                    kind, *pos = part
                    if part in PAIR_AT:
                        n = PAIR_AT[part]
                        if kind != "branch" or pos[0] % 2 == 0:
                            pe.wait_ge(landed[n % WRING], at(b, 16 * BUF_PAIRS[n % WRING], 16 * (n // WRING + 1)))
                        w = weights[:, n % WRING]
                    if part == ("kv",):
                        pe.wait_ge(xT_landed, at(b, 16, 16))
                    if isinstance(b, int) and part == ("turn", 0, 0):
                        pe.wait_ge(const_landed, 16)
                    if isinstance(b, int) and part == ("halves", 0):
                        pe.wait_ge(keys_landed, 16)
                    last = None
                    if kind in ("qa", "qr", "kr", "gate", "query", "kv", "vr", "gr"):
                        if part == ("query", 0):
                            for bank_emptied, turn in stands(b, *(("x1turn", t, i) for t in range(TILES) for i in range(2)), before=(*part, 0)):
                                pe.wait_ge(bank_emptied, turn)
                        pe.wait_ge(emptied[bank_no(*part, 0)], free(b, *part, 0))
                        bank = bank_of(*part, 0)
                        for u in range(2):
                            if kind in ("vr", "gr") or (kind == "kv" and u == 1):
                                for t in range(TILES):
                                    at_col = TILES + t if kind == "kv" else t * 2 + u
                                    o = bank[:, at_col * P:(at_col + 1) * P]
                                    for k in range(KD):
                                        last = pe.matmul(o, xT[:, k, t * P:t * P + P], w[:, u, k, :],
                                                         start=k == 0, stop=k == KD - 1)
                            else:
                                for k in range(KD):
                                    last = pe.matmul(bank[:, u * NT:u * NT + NT], w[:, u, k, :], xT[:, k, :],
                                                     start=k == 0, stop=k == KD - 1)
                        last.then_inc(bank_full, 1)
                    elif kind == "scores":
                        c, h = pos
                        if part == ("scores", 0, 0):
                            for bank_emptied, turn in stands(b, ("kv", 0), ("qa", 0, 0), ("qa", 1, 0), before=(*part, 0)):
                                pe.wait_ge(bank_emptied, turn)
                        half = slice(HD * h, HD * h + HD)
                        for i in range(2):
                            pe.wait_ge(emptied[bank_no(*part, i)], free(b, *part, i))
                            bank = bank_of(*part, i)
                            for j in range(2):
                                last = pe.matmul(bank[:, j * NT:(j + 1) * NT], qT[half, 2 * i + j, c * P:c * P + P],
                                                 kT[half, c:c + 2, :].rearrange("p a n -> p (a n)"),
                                                 start=True, stop=True)
                            last.then_inc(bank_full, 1)
                    elif kind == "turn":
                        c, h = pos
                        pe.wait_ge(probs_ready, at(b, 2 * KVH, c * KVH + h + 1))
                        for k in range(2):
                            pe.wait_ge(emptied[bank_no(*part, k)], free(b, *part, k))
                            bank = bank_of(*part, k)
                            for j in range(GROUP):
                                last = pe.transpose(bank[:, j * P:j * P + P], probs[:, j, k * P:k * P + P], ident)
                            last.then_inc(bank_full, 1)
                    elif kind == "pv":
                        c, h = pos
                        half = slice(HD * h, HD * h + HD)
                        for bank_emptied, turn in stands(b, ("turn", c, h, 0), ("turn", c, h, 1), before=(*part, 0)):
                            pe.wait_ge(bank_emptied, turn)
                        pe.wait_ge(emptied[bank_no(*part, 0)], free(b, *part, 0))
                        bank = bank_of(*part, 0)
                        for k in range(2):
                            last = pe.matmul(bank[half], v[:, c + k, half], probsT[:, k, :],
                                             start=k == 0, stop=k == 1)
                        last.then_inc(bank_full, 1)
                    elif kind == "ret_scores":
                        c = pos[0]
                        if c == 0:
                            for bank_emptied, turn in stands(b, *((m, i, 0) for m in ("qr", "kr") for i in range(2)), before=(*part, 0)):
                                pe.wait_ge(bank_emptied, turn)
                        tok = slice(c * P, c * P + P)
                        pe.wait_ge(emptied[bank_no(*part, 0)], free(b, *part, 0))
                        bank = bank_of(*part, 0)
                        for h in range(RH):
                            last = pe.matmul(bank[:, h * P:h * P + P], krT[:, h, tok], qrT[:, h, tok],
                                             start=True, stop=True)
                        last.then_inc(bank_full, 1)
                        pe.wait_ge(emptied[bank_no(*part, 1)], free(b, *part, 1))
                        bank = bank_of(*part, 1)
                        for h in range(RH):
                            last = pe.transpose(bank[:, h * P:h * P + P], krT[:, h, tok], ident)
                        last.then_inc(bank_full, 1)
                    elif kind == "ret_out":
                        c = pos[0]
                        if isinstance(b, int) and c == 0:
                            pe.wait_ge(state_zeroed, 1)
                        for bank_emptied, turn in stands(b, *((("vr", 0, 0), ("vr", 1, 0)) if c == 0 else (("ret_out", 0, 1),)), ("ret_scores", c, 0), ("ret_scores", c, 1), before=(*part, 0)):
                            pe.wait_ge(bank_emptied, turn)
                        pe.wait_ge(qd_ready, at(b, TILES, c + 1))
                        pe.wait_ge(emptied[bank_no(*part, 0)], free(b, *part, 0))
                        bank = bank_of(*part, 0)
                        for h in range(RH):
                            o = slice(h * P, h * P + P)
                            pe.matmul(bank[:, o], maskedT[:, o], vr[:, c, o], start=True, stop=False)
                            last = pe.matmul(bank[:, o], qd[:, h, :], state[:, o], start=False, stop=True)
                        last.then_inc(bank_full, 1)
                        pe.wait_ge(emptied[bank_no(*part, 1)], free(b, *part, 1))
                        bank = bank_of(*part, 1)
                        for h in range(RH):
                            o = slice(h * P, h * P + P)
                            last = pe.matmul(bank[:, o], kd[:, o], vr[:, c, o], start=True, stop=True)
                        last.then_inc(bank_full, 1)
                    elif kind == "ret_turn":
                        c = pos[0]
                        pe.wait_ge(ret_ready, at(b, TILES, c + 1))
                        pe.wait_ge(emptied[bank_no(*part, 0)], free(b, *part, 0))
                        bank = bank_of(*part, 0)
                        for h in range(RH):
                            last = pe.transpose(bank[:, h * P:h * P + P], ret[:, h * P:h * P + P], ident)
                        last.then_inc(bank_full, 1)
                    elif kind == "branch":
                        m = pos[0]
                        if m == 0:
                            for bank_emptied, turn in stands(b, *(("pv", c, h, 0) for c in range(TILES) for h in range(KVH)), *(("ret_turn", c, 0) for c in range(TILES)), before=(*part, 0)):
                                pe.wait_ge(bank_emptied, turn)
                        pe.wait_ge(emptied[bank_no(*part, 0)], free(b, *part, 0))
                        bank = bank_of(*part, 0)
                        for side, src in enumerate((attnT, retT)):
                            for k in range(4):
                                last = pe.matmul(bank[:, side * NT:side * NT + NT], w[:, m % 2, side * 4 + k, :],
                                                 src[:, k, :], start=k == 0, stop=k == 3)
                        last.then_inc(bank_full, 1)
                    elif kind == "out":
                        if pos[0] == 0:
                            for bank_emptied, turn in stands(b, *(("branch", m, 0) for m in range(KD)), before=(*part, 0)):
                                pe.wait_ge(bank_emptied, turn)
                        pe.wait_ge(emptied[bank_no(*part, 0)], free(b, *part, 0))
                        bank = bank_of(*part, 0)
                        for u in range(2):
                            for t in range(TILES):
                                o = bank[:, (t * 2 + u) * P:(t * 2 + u + 1) * P]
                                for k in range(KD):
                                    last = pe.matmul(o, merged[:, k, t * P:t * P + P], w[:, u, k, :],
                                                     start=k == 0, stop=k == KD - 1)
                        last.then_inc(bank_full, 1)
                    elif kind == "x1turn":
                        t = pos[0]
                        pe.wait_ge(x1_ready, at(b, TILES, t + 1))
                        for i in range(2):
                            pe.wait_ge(emptied[bank_no(*part, i)], free(b, *part, i))
                            bank = bank_of(*part, i)
                            for k in range(4):
                                last = pe.transpose(bank[:, k * P:k * P + P],
                                                    x1n[:, t, (4 * i + k) * P:(4 * i + k + 1) * P], ident)
                            last.then_inc(bank_full, 1)
                    elif kind == "halves":
                        h = pos[0]
                        for bank_emptied, turn in stands(b, ("query", h, 0), before=(*part, 0)):
                            pe.wait_ge(bank_emptied, turn)
                        pe.wait_ge(emptied[bank_no(*part, 0)], free(b, *part, 0))
                        bank = bank_of(*part, 0)
                        for t in range(TILES):
                            for half in range(2):
                                last = pe.matmul(bank[:, (t * 2 + half) * P:(t * 2 + half + 1) * P],
                                                 queryT[:, half, t * P:t * P + P], keys[:, half, :],
                                                 start=True, stop=True)
                        last.then_inc(bank_full, 1)
                    yield

            def up(b, g):
                t, s0 = g // TGROUPS, (g % TGROUPS) * PAIR
                if g % TGROUPS == 0 and started(b):
                    pe.wait_ge(acc_read, at(b, TILES, t - 1))
                pe.wait_ge(diag_ready, at(b, GROUPS, g + 1))
                for i in range(PAIR):
                    buf = buffer(g, i)
                    for n in range(2):
                        last = pe.matmul(acc[:, t, n * 512:n * 512 + 512], diag[:, g % 2, i, :],
                                         rows[:, buf, 1, n * 512:n * 512 + 512],
                                         start=s0 + i == 0, stop=s0 + i == SLOTS - 1, skip_group_check=True)
                last.then_inc(up_done, 1)

            def head(b):
                if started(b):
                    up(b - 1, GROUPS - 1)
                for g in range(HEAD - 1):
                    up(b, g)

            def body(b, mix):
                done = [0]
                for g in range(HEAD, GROUPS):
                    if mix:
                        spread(g, mix, done, ahead=True)
                    up(b, g - 1)

            for _ in mixer(0):
                pass
            head(0)
            with pe.Fori(0, BLOCKS - 1) as b:
                body(b, mixer(b + 1))
                head(b + 1)
            body(BLOCKS - 1, None)
            up(BLOCKS - 1, GROUPS - 1)

        @block.vector
        def _(dve):
            def mixer(b, parts=PARTS):
                chain = 0 if parts is PARTS else MIX_STEPS

                def count():
                    nonlocal chain
                    chain += 1
                    return at(b, MIX_STEPS + TAIL_STEPS, chain)

                def top16(vals, ids, src, scratch):
                    dve.max(vals[:, 0:8], src).then_inc(mix_step, 1)
                    dve.wait_ge(mix_step, count())
                    settle(dve)
                    dve.max_index(ids[:, 0:8], vals[:, 0:8], src)
                    dve.match_replace(scratch, vals[:, 0:8], src, LOWEST).then_inc(mix_step, 1)
                    dve.wait_ge(mix_step, count())
                    settle(dve)
                    dve.max(vals[:, 8:16], scratch).then_inc(mix_step, 1)
                    dve.wait_ge(mix_step, count())
                    settle(dve)
                    return dve.max_index(ids[:, 8:16], vals[:, 8:16], scratch)

                def combine(t, h):
                    sums = cand[:, h % 2, :]
                    dve.tensor_tensor(sums.rearrange("p (i j) -> p i j", i=TOPK),
                                      val[:, t, 0, h].unsqueeze(2).to_broadcast([P, TOPK, TOPK]),
                                      val[:, t, 1, h].unsqueeze(1).to_broadcast([P, TOPK, TOPK]), ALU.add).then_inc(mix_step, 1)
                    dve.wait_ge(mix_step, count())
                    settle(dve)
                    top16(topv[:, h, :], topp[:, h * TOPK:(h + 1) * TOPK], sums, rest[:, 0, :]).then_inc(mix_step, 1)
                    dve.wait_ge(mix_step, count())
                    settle(dve)

                for part in parts:
                    kind, *pos = part
                    first = isinstance(b, int) and b == 0
                    if kind == "kv":
                        dve.wait_ge(bank_full, filled(b, *part, 0))
                        bank = bank_of(*part, 0)
                        dve.tensor_copy(kT[:, 0, :], kT[:, 2, :])
                        dve.tensor_copy(v[:, 0, :], v[:, 2, :]).then_inc(mix_step, 1)
                        dve.wait_ge(mix_step, count())
                        dve.tensor_copy(kT[:, 1:3, :].rearrange("p a n -> p (a n)"), bank[:, 0:NT])
                        dve.tensor_copy(v[:, 1:3, :].rearrange("p a n -> p (a n)"), bank[:, NT:]).then_inc(emptied[bank_no(*part, 0)], 1)
                    elif kind == "scores":
                        c, h = pos
                        lo = P if first and c == 0 else 0
                        if first and (c, h) == (0, 0):
                            dve.wait_ge(const_landed, 16)
                            dve.wait_ge(par_landed, 16)
                        for i in range(2):
                            dve.wait_ge(bank_full, filled(b, *part, i))
                            bank = bank_of(*part, i)
                            for j in range(2):
                                ins = dve.scalar_tensor_tensor(
                                    out=probs[:, 2 * i + j, lo:], in0=dist[:, lo:], scalar=-slopes[h * GROUP + 2 * i + j],
                                    in1=bank[:, j * NT + lo:(j + 1) * NT], op0=ALU.mult, op1=ALU.add)
                            ins.then_inc(emptied[bank_no(*part, i)], 1)
                        for bank_emptied, turn in stands(b, (*part, 0), (*part, 1)):
                            dve.wait_ge(bank_emptied, turn)
                        dve.tensor_reduce(small[:, 0:4], probs[:, :, lo:], AX, ALU.max).then_inc(mix_step, 1)
                        dve.wait_ge(mix_step, count())
                        sinks = par[:, R_SINK + h * GROUP:R_SINK + (h + 1) * GROUP]
                        dve.tensor_tensor(small[:, 0:4], small[:, 0:4], sinks, ALU.max).then_inc(mix_step, 1)
                        dve.wait_ge(mix_step, count())
                        dve.tensor_scalar(small[:, 4:8], small[:, 0:4], -1.0, None, ALU.mult)
                        dve.tensor_tensor(small[:, 8:12], sinks, small[:, 0:4], ALU.subtract).then_inc(max_ready, 1)
                        dve.wait_ge(exp_done, at(b, 2 * KVH, c * KVH + h + 1))
                        dve.tensor_tensor(small[:, 20:24], small[:, 12:16], small[:, 16:20], ALU.add).then_inc(mix_step, 1)
                        dve.wait_ge(mix_step, count())
                        dve.reciprocal(small[:, 24:28], small[:, 20:24]).then_inc(mix_step, 1)
                        dve.wait_ge(mix_step, count())
                        for j in range(GROUP):
                            ins = dve.tensor_scalar(probs[:, j, lo:], probs[:, j, lo:], small[:, 24 + j:25 + j], None,
                                                    ALU.mult)
                        ins.then_inc(probs_ready, 1)
                    elif kind == "vr":
                        i = pos[0]
                        dve.wait_ge(bank_full, filled(b, *part, 0))
                        bank = bank_of(*part, 0)
                        dve.tensor_copy(vr[:, :, i * NT:i * NT + NT],
                                              bank.rearrange("p (t n) -> p t n", t=TILES)).then_inc(emptied[bank_no(*part, 0)], 1)
                    elif kind == "gr":
                        i = pos[0]
                        dve.wait_ge(bank_full, filled(b, *part, 0))
                        bank = bank_of(*part, 0)
                        e = gates[:, i % 2].rearrange("p a n -> p (a n)")
                        dve.wait_ge(swish_exp, at(b, 2, i + 1))
                        dve.tensor_scalar(e, e, 1.0, None, ALU.add).then_inc(mix_step, 1)
                        dve.wait_ge(mix_step, count())
                        dve.reciprocal(e, e).then_inc(mix_step, 1)
                        dve.wait_ge(mix_step, count())
                        dve.tensor_tensor(
                            swish[:, :, i * NT:i * NT + NT], bank.rearrange("p (t n) -> p t n", t=TILES),
                            e.rearrange("p (t n) -> p t n", t=TILES), ALU.mult).then_inc(mix_step, 1)
                        dve.wait_ge(mix_step, count())
                        gain = par[:, R_GN + i * NT:R_GN + i * NT + NT].unsqueeze(1).to_broadcast([P, TILES, NT])
                        dve.tensor_tensor(swish[:, :, i * NT:i * NT + NT], swish[:, :, i * NT:i * NT + NT],
                                                gain, ALU.mult).then_inc(emptied[bank_no(*part, 0)], 1)
                    elif kind == "gate":
                        m = pos[0]
                        for bank_emptied, turn in stands(b, (*part, 0)):
                            dve.wait_ge(bank_emptied, turn)
                        e = gates[:, m % 2].rearrange("p a n -> p (a n)")
                        dve.tensor_scalar(e, e, 1.0, None, ALU.add).then_inc(mix_step, 1)
                        dve.wait_ge(mix_step, count())
                        dve.reciprocal(e, e).then_inc(mix_step, 1)
                        dve.wait_ge(mix_step, count())
                    elif kind == "ret_scores":
                        c = pos[0]
                        dve.wait_ge(bank_full, filled(b, *part, 0))
                        bank = bank_of(*part, 0)
                        dve.tensor_tensor(maskedT[:, :], bank, rmask, ALU.mult).then_inc(emptied[bank_no(*part, 0)], 1)
                        dve.wait_ge(bank_full, filled(b, *part, 1))
                        bank = bank_of(*part, 1)
                        dve.tensor_tensor(kd[:, :].rearrange("p (h n) -> p h n", h=RH),
                                                bank.rearrange("p (h n) -> p h n", h=RH),
                                                kdec.unsqueeze(2).to_broadcast([P, RH, P]), ALU.mult).then_inc(emptied[bank_no(*part, 1)], 1)
                        for bank_emptied, turn in stands(b, ("qr", 0, 0), ("qr", 1, 0)):
                            dve.wait_ge(bank_emptied, turn)
                        dve.tensor_tensor(qd[:, :, :], qrT[:, :, c * P:c * P + P], qdec, ALU.mult).then_inc(qd_ready, 1)
                    elif kind == "ret_out":
                        c = pos[0]
                        dve.wait_ge(bank_full, filled(b, *part, 0))
                        bank = bank_of(*part, 0)
                        for h in range(RH):
                            ins = dve.bn_stats(stats[:, h, :], bank[:, h * P:h * P + P])
                        ins.then_inc(mix_step, 1)
                        dve.wait_ge(mix_step, count())
                        settle(dve)
                        for h in range(RH):
                            ins = dve.bn_aggr(mv[:, h, :], stats[:, h, :])
                        ins.then_inc(mix_step, 1)
                        dve.wait_ge(mix_step, count())
                        dve.tensor_copy(variance[:, :], mv[:, :, 1]).then_inc(mix_step, 1)
                        dve.wait_ge(mix_step, count())
                        inverse_root(mix_step, count, rstd[:, :], variance[:, :], roottmp[:, :])
                        for h in range(RH):
                            ins = dve.tensor_scalar(ret[:, h * P:h * P + P], bank[:, h * P:h * P + P], mv[:, h, 0:1],
                                                    rstd[:, h:h + 1], ALU.subtract, ALU.mult)
                        ins.then_inc(emptied[bank_no(*part, 0)], 1)
                        for bank_emptied, turn in stands(b, (*part, 0), ("gr", 0, 0), ("gr", 1, 0)):
                            dve.wait_ge(bank_emptied, turn)
                        dve.tensor_tensor(ret[:, :], ret[:, :], swish[:, c, :], ALU.mult).then_inc(ret_ready, 1)
                        dve.wait_ge(bank_full, filled(b, *part, 1))
                        bank = bank_of(*part, 1)
                        for h in range(RH):
                            o = slice(h * P, h * P + P)
                            ins = dve.scalar_tensor_tensor(out=state[:, o], in0=state[:, o], scalar=chunk_decay[h],
                                                           in1=bank[:, o], op0=ALU.mult, op1=ALU.add)
                        ins.then_inc(emptied[bank_no(*part, 1)], 1)
                    elif kind == "branch":
                        m = pos[0]
                        dve.wait_ge(bank_full, filled(b, *part, 0))
                        bank = bank_of(*part, 0)
                        g = gates[:, m % 2].rearrange("p a n -> p (a n)")
                        dve.tensor_tensor(g, g, bank, ALU.mult).then_inc(mix_step, 1)
                        dve.wait_ge(mix_step, count())
                        ins = dve.tensor_tensor(merged[:, m, :], g[:, 0:NT], g[:, NT:], ALU.add)
                        ins.then_inc(emptied[bank_no(*part, 0)], 1)
                    elif kind == "out":
                        n = pos[0]
                        if n == 0:
                            dve.wait_ge(xn_landed, at(b, 16, 16))
                        dve.wait_ge(bank_full, filled(b, *part, 0))
                        bank = bank_of(*part, 0)
                        to = x1n[:, :, n * NT:n * NT + NT]
                        dve.scalar_tensor_tensor(out=to, in0=to, scalar=ALPHA,
                                                       in1=bank.rearrange("p (t n) -> p t n", t=TILES),
                                                       op0=ALU.mult, op1=ALU.add).then_inc(emptied[bank_no(*part, 0)], 1)
                    elif kind == "norm":
                        t = pos[0]
                        for bank_emptied, turn in stands(b, *(("out", n, 0) for n in range(4))):
                            dve.wait_ge(bank_emptied, turn)
                        for i in range(2):
                            ins = dve.bn_stats(stats[:, i, :], x1n[:, t, i * 512:i * 512 + 512])
                        ins.then_inc(mix_step, 1)
                        dve.wait_ge(mix_step, count())
                        settle(dve)
                        dve.bn_aggr(mv[:, 0, :], stats[:, 0:2, :].rearrange("p a s -> p (a s)")).then_inc(mix_step, 1)
                        dve.wait_ge(mix_step, count())
                        inverse_root(mix_step, count, rstd[:, 0:1], mv[:, 0, 1:2], roottmp[:, 0:1])
                        dve.tensor_scalar(x1n[:, t, :], x1n[:, t, :], mv[:, 0, 0:1], rstd[:, 0:1],
                                               ALU.subtract, ALU.mult).then_inc(mix_step, 1)
                        dve.wait_ge(mix_step, count())
                        dve.tensor_tensor(x1n[:, t, :], x1n[:, t, :], par[:, R_MG:R_MB], ALU.mult).then_inc(mix_step, 1)
                        dve.wait_ge(mix_step, count())
                        dve.tensor_tensor(x1n[:, t, :], x1n[:, t, :], par[:, R_MB:R_FG], ALU.add).then_inc(x1_ready, 1)
                    elif kind == "halves":
                        h = pos[0]
                        dve.wait_ge(scores_kept, at(b, PH, h + 1))
                        bank = bank_of(*part, 0)
                        settle(dve)
                        for half in range(2):
                            ins = top16(val[:, 0, half, h, :], idx[:, 0, half, h, :],
                                        bank[:, half * NK:(half + 1) * NK], rest[:, half, 0:NK])
                        ins.then_inc(emptied[bank_no(*part, 0)], 1)
                        combine(0, h)
                    elif kind == "rank":
                        h = pos[0]
                        for half in range(2):
                            top16(val[:, 1, half, h, :], idx[:, 1, half, h, :], kept[:, h, half, :],
                                  rest[:, half, 0:NK])
                        combine(1, h)
                    elif kind == "pick":
                        t, s, side = pos
                        if (s, side) == ("rows", 0):
                            dve.tensor_copy(idxf[:, :, :], idx[:, t].rearrange("p a h k -> p a (h k)")).then_inc(mix_step, 1)
                            dve.wait_ge(mix_step, count())
                        if s in ("rows", "columns"):
                            a = int(s == "columns")
                            slots = slice(side * SLOTS // 2, (side + 1) * SLOTS // 2)
                            dve.tensor_scalar(posu[:, a, slots], topp[:, slots], *((4, None, ALU.logical_shift_right)
                                              if a == 0 else (TOPK - 1, None, ALU.bitwise_and))).then_inc(mix_step, 1)
                            dve.wait_ge(mix_step, count())
                            dve.tensor_copy(posf[:, a, slots], posu[:, a, slots]).then_inc(mix_step, 1)
                            dve.wait_ge(mix_step, count())
                            dve.tensor_tensor(onehot, posf[:, a, slots].unsqueeze(2).to_broadcast([P, SLOTS // 2, TOPK]),
                                              iota.unsqueeze(1).to_broadcast([P, SLOTS // 2, TOPK]), ALU.is_equal).then_inc(mix_step, 1)
                            dve.wait_ge(mix_step, count())
                            hot = onehot.rearrange("p (h s) a -> p h s a", h=PH // 2)
                            ids = idxf[:, a, slots].rearrange("p (h a) -> p h a", h=PH // 2)
                            dve.tensor_tensor(hot, hot, ids.unsqueeze(2).to_broadcast([P, PH // 2, TOPK, TOPK]), ALU.mult).then_inc(mix_step, 1)
                            dve.wait_ge(mix_step, count())
                            dve.tensor_reduce(part_e[:, a, slots], onehot, AX, ALU.add).then_inc(mix_step, 1)
                            dve.wait_ge(mix_step, count())
                        else:
                            dve.scalar_tensor_tensor(out=expert_next[:, t, :], in0=part_e[:, 0, :], scalar=float(NK),
                                                     in1=part_e[:, 1, :], op0=ALU.mult, op1=ALU.add)
                            dve.tensor_copy(gsum[:, 0, :], topv[:, :, 0]).then_inc(mix_step, 1)
                            dve.wait_ge(mix_step, count())
                            dve.tensor_tensor(topv[:, :, :], topv[:, :, :],
                                              gsum[:, 0, :].unsqueeze(2).to_broadcast([P, PH, TOPK]),
                                              ALU.subtract).then_inc(gdiff_ready, 1)
                            dve.wait_ge(gexp_done, at(b, TILES, t + 1))
                            dve.tensor_reduce(gsum[:, 0, :], topv[:, :, :], AX, ALU.add).then_inc(mix_step, 1)
                            dve.wait_ge(mix_step, count())
                            dve.reciprocal(gsum[:, 1, :], gsum[:, 0, :]).then_inc(mix_step, 1)
                            dve.wait_ge(mix_step, count())
                            dve.tensor_tensor(gate_next[:, t, :].rearrange("p (h k) -> p h k", h=PH), topv[:, :, :],
                                                   gsum[:, 1, :].unsqueeze(2).to_broadcast([P, PH, TOPK]), ALU.mult).then_inc(mix_step, 1)
                            dve.wait_ge(mix_step, count())
                    elif kind == "publish":
                        publish(0)
                    if part == parts[-1]:
                        assert chain == (MIX_STEPS if parts is PARTS else MIX_STEPS + TAIL_STEPS), chain
                    yield

            def inverse_root(step, count, out, var, tmp):
                dve.tensor_scalar(var, var, EPS, None, ALU.add).then_inc(step, 1)
                dve.wait_ge(step, count())
                dve.tensor_scalar(tmp.bitcast(U32), var.bitcast(U32), 1, None, ALU.logical_shift_right).then_inc(step, 1)
                dve.wait_ge(step, count())
                dve.tensor_scalar(out.bitcast(U32), tmp.bitcast(U32), -1.0, float(0x5F3759DF), ALU.mult, ALU.add).then_inc(step, 1)
                dve.wait_ge(step, count())
                for _ in range(3):
                    dve.scalar_tensor_tensor(out=tmp, in0=out, scalar=-0.5, in1=out, op0=ALU.mult, op1=ALU.mult).then_inc(step, 1)
                    dve.wait_ge(step, count())
                    dve.tensor_tensor(tmp, tmp, var, ALU.mult).then_inc(step, 1)
                    dve.wait_ge(step, count())
                    dve.scalar_tensor_tensor(out=out, in0=tmp, scalar=1.5, in1=out, op0=ALU.add, op1=ALU.mult).then_inc(step, 1)
                    dve.wait_ge(step, count())

            def publish(t):
                dve.tensor_copy(gate[:, t, :], gate_next[:, t, :])
                dve.tensor_copy(x1[:, t, :], x1n[:, t, :])
                dve.tensor_copy(expert[:, t, :], expert_next[:, t, :]).then_inc(published, 1)

            def finish(b, t):
                n = 0

                def count():
                    nonlocal n
                    n += 1
                    return at(b, FIN_STEPS * TILES, FIN_STEPS * t + n)

                dve.wait_ge(up_done, at(b, GROUPS, TGROUPS * (t + 1)))
                dve.wait_ge(stored, at(b, 16 * TILES, 16 * (t + 1)))
                dve.scalar_tensor_tensor(out=y[:, :], in0=x1[:, t, :], scalar=ALPHA, in1=acc[:, t, :],
                                         op0=ALU.mult, op1=ALU.add).then_inc(acc_read, 1)
                yield
                dve.wait_ge(acc_read, at(b, TILES, t + 1))
                for i in range(2):
                    ins = dve.bn_stats(fstats[:, i, :], y[:, i * 512:i * 512 + 512])
                ins.then_inc(fin_step, 1)
                dve.wait_ge(fin_step, count())
                settle(dve)
                dve.bn_aggr(fmv[:, :], fstats[:, :, :].rearrange("p a s -> p (a s)")).then_inc(fin_step, 1)
                dve.wait_ge(fin_step, count())
                inverse_root(fin_step, count, frstd[:, :], fmv[:, 1:2], roottmp[:, 0:1])
                yield
                dve.tensor_scalar(y[:, :], y[:, :], fmv[:, 0:1], frstd[:, 0:1], ALU.subtract, ALU.mult).then_inc(fin_step, 1)
                dve.wait_ge(fin_step, count())
                dve.tensor_tensor(y[:, :], y[:, :], par[:, R_FG:R_FB], ALU.mult).then_inc(fin_step, 1)
                dve.wait_ge(fin_step, count())
                dve.tensor_tensor(y[:, :], y[:, :], par[:, R_FB:R_GN], ALU.add).then_inc(out_ready, 1)
                assert n == FIN_STEPS
                yield

            MIX_STEPS, TAIL_STEPS, FIN_STEPS = 222, 113, 16

            def dots(b, g):
                t = g // TGROUPS
                for i in range(PAIR):
                    buf = buffer(g, i)
                    dve.wait_ge(gathered[buf], arrived(b, g))
                    ins = dve.tensor_tensor_reduce(rows[:, buf, 0, :], rows[:, buf, 0, :], x1[:, t, :], 1.0, 0.0,
                                                   ALU.mult, ALU.add, hdot[:, g % 2, i:i + 1])
                ins.then_inc(dots_done, 1)

            def diagonals(b, g):
                t, s0 = g // TGROUPS, (g % TGROUPS) * PAIR
                dve.wait_ge(gelu_done, at(b, GROUPS, g + 1))
                if g > 1 or started(b):
                    dve.wait_ge(up_done, at(b, GROUPS, g - 1))
                for i in range(PAIR):
                    ins = dve.tensor_scalar(diag[:, g % 2, i, :], ident, hact[:, g % 2, i:i + 1],
                                            gate[:, t, s0 + i:s0 + i + 1], ALU.mult, ALU.mult)
                ins.then_inc(diag_ready, 1)

            def head(b):
                output = finish(b - 1, 1) if started(b) else None
                for g in range(HEAD):
                    dots(b, g)
                    if g:
                        diagonals(b, g - 1)
                    elif started(b):
                        diagonals(b - 1, GROUPS - 1)
                    if output and 2 <= g <= 4:
                        next(output)

            def body(b, mix):
                done = [0]
                tail = mixer(b, TAIL)
                output = finish(b, 0)
                for g in range(HEAD, GROUPS):
                    dots(b, g)
                    diagonals(b, g - 1)
                    if g in TAIL_AT:
                        next(tail)
                    if g == TAIL_END:
                        publish(1)
                    if mix:
                        spread(g - 1, mix, done)
                    if TGROUPS + 2 <= g <= TGROUPS + 4:
                        next(output)

            for bank in range(BANKS):
                dve.sem_inc(emptied[bank], 1)
            dve.memset(small[:, :], 0.0)
            dve.memset(probs[:, :, :], 0.0)
            dve.memset(kT[:, 2, :], 0.0)
            dve.memset(v[:, 2, :], 0.0)
            dve.memset(state[:, :], 0.0).then_inc(state_zeroed, 1)
            dve.wait_ge(state_zeroed, 1)
            for _ in mixer(0):
                pass
            head(0)
            with dve.Fori(0, BLOCKS - 1) as b:
                body(b, mixer(b + 1))
                head(b + 1)
            body(BLOCKS - 1, None)
            diagonals(BLOCKS - 1, GROUPS - 1)
            for _ in finish(BLOCKS - 1, 1):
                pass


def kernel(**inputs):
    import numpy as _np
    import concourse.bacc as _bacc
    from concourse import mybir as _mybir
    from concourse.bass_utils import run_bass_kernel_spmd as _run

    a = {k: _np.asarray(v) for k, v in inputs.items()}
    x = a["x"][0]
    splits = _np.cumsum([0, AH * HD, KVH * HD, KVH * HD, RH * P, RH * P, RH * P, RH * P, D, D])
    qa, ka, va, qr, kr, vr, gr, ga, gb = (a["w_in"][0][:, splits[i]:splits[i + 1]] for i in range(9))

    def unit(w):
        return w.reshape(-1, P, P).transpose(1, 0, 2)

    heads = _np.concatenate([_np.r_[j * HD:(j + 1) * HD, (j + GROUP) * HD:(j + GROUP + 1) * HD] for j in range(GROUP)])
    qa = qa[:, heads]
    wa, wr = a["w_attn_branch"][0][heads], a["w_ret_branch"][0]
    wo, wq = a["w_out"][0], a["w_peer_query"][0]

    def col(w, n):
        return unit(w[:, n * P:(n + 1) * P])

    def pair(p):
        kind, i = p[0], p[1] if len(p) > 1 else 0
        if kind == "kv":
            return col(ka, 0), col(va, 0)
        if kind == "gate":
            return col(ga, i), col(gb, i)
        if kind == "branch":
            return tuple(_np.concatenate([col(wa, m), col(wr, m)], axis=1) for m in (i, i + 1))
        w = {"qa": qa, "qr": qr, "kr": kr, "vr": vr, "gr": gr, "out": wo, "query": wq}[kind]
        return col(w, 2 * i), col(w, 2 * i + 1)

    weights = _np.stack([_np.stack(pair(p), axis=1).reshape(P, 2 * D) for p in PAIRS])
    par = _np.concatenate([a[n][0] for n in ("ln_mix_gain", "ln_mix_bias", "ln_ffn_gain", "ln_ffn_bias",
                                             "ret_gn_gain", "attn_sinks")])
    arrays = {
        "xT_dram": x.T.reshape(KD, P, BLOCKS, NT).transpose(2, 1, 0, 3),
        "xn_dram": x.reshape(BLOCKS, TILES, P, D).transpose(0, 2, 1, 3),
        "weights_dram": weights,
        "keys_dram": a["peer_sub_keys"][0].transpose(2, 0, 1),
        "const_dram": constants(),
        "par_dram": _np.broadcast_to(par, (P, len(par))),
        "rows_dram": _np.concatenate([a["peer_down"][0], a["peer_up"][0]], axis=1),
    }
    arrays = {k: _np.ascontiguousarray(v) for k, v in arrays.items()}
    nc = _bacc.Bacc("TRN2", target_bir_lowering=False, num_devices=1)
    args = [nc.dram_tensor(k, v.shape, _mybir.dt.from_np(v.dtype), kind="ExternalInput").ap()
            for k, v in arrays.items()]
    out = nc.dram_tensor("out_dram", (BLOCKS, TILES, P, D), F32, kind="ExternalOutput").ap()
    build(nc, *args, out)
    r = _run(nc, [arrays], core_ids=[0])
    return r.results[0]["out_dram"].reshape(1, S, D)
```

```python
from contextlib import ExitStack

import concourse.bass as bass
import numpy as np
from concourse import mybir

F32 = mybir.dt.float32
U32 = mybir.dt.uint32
ALU = mybir.AluOpType
ACT = mybir.ActivationFunctionType
AX = mybir.AxisListType.X

P = 128
D = 1024
KD = D // P
S = 1024
TILES = 2
NT = TILES * P
BLOCKS = S // NT
HD, KVH, GROUP = 64, 2, 4
AH = KVH * GROUP
RH = 4
PH, TOPK, NK = 8, 16, 128
SLOTS = PH * TOPK
ALPHA = float(2.0 ** 0.25)
EPS = 1e-5
FAR = 1.0e30
LOWEST = -3.0e38

RING = 10
PAIR = 2
GROUPS = TILES * SLOTS // PAIR
TGROUPS = SLOTS // PAIR
DEPTH = 4
_ROUNDS = -(-GROUPS // (RING // PAIR))
_SHORT = _ROUNDS * (RING // PAIR) - GROUPS
PLACE = [j for r in range(_ROUNDS) for j in range(RING // PAIR - ((r + 1) * _SHORT // _ROUNDS > r * _SHORT // _ROUNDS))]
WRING = 2
KEPT = 3
BANKS = 4

QUARTER = SLOTS // 4
PARTS = (
    [("kv",), ("qa", 0), ("qa", 1), ("scores", 0, 0), ("probs", 0, 0), ("qr", 0),
     ("turn", 0, 0), ("scores", 0, 1), ("probs", 0, 1), ("qr", 1), ("pv", 0, 0), ("turn", 0, 1), ("scores", 1, 0),
     ("probs", 1, 0), ("kr", 0), ("pv", 0, 1), ("turn", 1, 0), ("scores", 1, 1), ("probs", 1, 1), ("kr", 1),
     ("pv", 1, 0), ("turn", 1, 1), ("vr", 0), ("pv", 1, 1), ("vr", 1),
     ("gr", 0), ("ret_scores", 0), ("gr", 1), ("ret_out", 0), ("ret_scores", 1), ("gate", 0),
     ("ret_turn", 0), ("ret_out", 1), ("gate", 1), ("ret_turn", 1)]
    + [p for m in range(0, KD, 2)
       for p in ([("gate", m), ("gate", m + 1)] if m else []) + [("branch", m), ("branch", m + 1)]]
    + [("out", n) for n in range(4)] + [("norm", 0), ("norm", 1), ("x1turn", 0), ("x1turn", 1)]
    + [p for h in range(PH) for p in [("query", h), ("halves", h)] + ([("pick", 0, h // 2)] if h % 2 else [])]
    + [("softmax", 0), ("gates", 0), ("publish",)]
)
TAIL = tuple([p for h in range(PH) for p in [("rank", h)] + ([("pick", 1, h // 2)] if h % 2 else [])]
             + [("softmax", 1), ("gates", 1)])
HEAD = 5
TAIL_AT = [HEAD + 2 * n for n in range(len(TAIL))]
TAIL_END = TAIL_AT[-1] + 1
AHEAD = 3
MIX_END = GROUPS - 7
_EFFORT = dict.fromkeys(("kv", "qa", "qr", "kr", "vr", "gr", "gate", "out", "query"), 5) | dict.fromkeys(
    ("branch", "ret_out", "norm"), 3) | dict.fromkeys(("scores", "halves", "pick"), 2)
EFFORT = np.cumsum([_EFFORT.get(p[0], 1) for p in PARTS]).tolist()
PAIRS = [p for p in PARTS if p[0] in ("kv", "qa", "qr", "kr", "vr", "gr", "gate", "out", "query")
         or (p[0] == "branch" and p[1] % 2 == 0)]
PAIR_AT = {p: n for n, p in enumerate(PAIRS)}
for _m in range(1, KD, 2):
    PAIR_AT[("branch", _m)] = PAIR_AT[("branch", _m - 1)]
USES = []
for _p in PARTS:
    _n = 2 if _p[0] in ("scores", "turn", "ret_scores", "ret_out", "x1turn") else (
        0 if _p[0] in ("norm", "pick", "softmax", "gates", "probs", "publish") else 1)
    USES += [(*_p, i) for i in range(_n)]
USE_AT = {u: n for n, u in enumerate(USES)}
STREAM = PAIRS[KEPT:]
LAST_USE = [USE_AT[(p[0], p[1] + 1, 0) if p[0] == "branch" else (*p, 0)] for p in STREAM]
BANK_USES = [len(range(b, len(USES), BANKS)) for b in range(BANKS)]
BUF_PAIRS = [len(range(b, len(STREAM), WRING)) for b in range(WRING)]

C_IDENT, C_DIST, C_RMASK, C_QDEC, C_KDEC, C_IOTA, C_END = np.cumsum([0, P, 2 * P, RH * P, RH * P, RH, TOPK]).tolist()
R_MG, R_MB, R_FG, R_FB, R_GN, R_SINK, R_END = np.cumsum([0, D, D, D, D, RH * P, AH]).tolist()


def log_gammas():
    return np.log1p(-(2.0 ** (-5.0 - np.arange(RH, dtype=np.float32)))).astype(np.float32)


def constants():
    c = np.zeros((P, C_END), np.float32)
    c[:, C_IDENT:C_DIST] = np.eye(P)
    dist = (np.arange(P)[:, None] + P) - np.arange(2 * P)[None, :]
    c[:, C_DIST:C_RMASK] = np.where((dist >= 0) & (dist < P), dist, FAR)
    lg = log_gammas()
    pos = np.arange(P, dtype=np.float32)
    for h in range(RH):
        diff = pos[None, :] - pos[:, None]
        c[:, C_RMASK + h * P:C_RMASK + (h + 1) * P] = np.where(diff >= 0, np.exp(np.maximum(diff, 0) * lg[h]), 0)
        c[:, C_QDEC + h * P:C_QDEC + (h + 1) * P] = np.exp((pos + 1) * lg[h])[None, :]
        c[:, C_KDEC + h] = np.exp((P - 1 - pos) * lg[h])
    c[:, C_IOTA:C_END] = np.arange(TOPK)[None, :]
    return c


def build(nc, xT_d, xn_d, w_d, keys_d, const_d, par_d, rows_d, out_d):
    slopes = [float(2.0 ** (-8.0 * (h + 1) / AH)) for h in range(AH)]
    chunk_decay = [float(np.exp(np.float32(P) * g)) for g in log_gammas()]
    with ExitStack() as ctx:
        def sb(name, shape, dt=F32):
            return ctx.enter_context(nc.sbuf_tensor(name, shape, dt))

        def sem(name):
            return ctx.enter_context(nc.semaphore(name))

        ps = ctx.enter_context(nc.psum_tensor("ps", [P, 8, 512], F32))
        acc = ps[:, BANKS:8, :].rearrange("p (t a) b -> p t (a b)", t=TILES)

        const = sb("const", [P, C_END])
        ident = const[:, C_IDENT:C_DIST]
        dist = const[:, C_DIST:C_RMASK]
        rmask = const[:, C_RMASK:C_QDEC]
        qdec = const[:, C_QDEC:C_KDEC].rearrange("p (h i) -> p h i", h=RH)
        kdec = const[:, C_KDEC:C_IOTA]
        iota = const[:, C_IOTA:C_END]
        par = sb("par", [P, R_END])
        keys = sb("keys", [P, 2, NK])
        weights = sb("weights", [P, WRING, 2, KD, P])
        kept_weights = sb("kept_weights", [P, KEPT, 2, KD, P])
        rows = sb("rows", [P, RING, 2, D])
        xT = sb("xT", [P, KD, NT])
        x1n = sb("x1n", [P, TILES, D])
        qrT = x1n[:, 0, :].rearrange("p (h n) -> p h n", h=RH)
        krT = x1n[:, 1, :].rearrange("p (h n) -> p h n", h=RH)
        kT = sb("kT", [P, 3, P])
        v = sb("v", [P, 3, P])
        vr = sb("vr", [P, TILES, RH * P])
        pick8k = sb("pick8k", [P, 2, D])
        probs = pick8k[:, 0, :].rearrange("p (j s) -> p j s", j=GROUP)
        probsT = pick8k[:, 1, :].rearrange("p (k n) -> p k n", k=2)
        cand = pick8k[:, 0, 0:2 * TOPK * TOPK].rearrange("p (h c) -> p h c", h=2)
        attnT = sb("attnT", [P, GROUP, NT])
        gates = pick8k[:, 0, :].rearrange("p (i a n) -> p i a n", i=2, a=2)
        retT = pick8k[:, 1, :].rearrange("p (h n) -> p h n", h=RH)
        maskedT = sb("maskedT", [P, RH * P])
        ret = sb("ret", [P, RH * P])
        state = sb("state", [P, RH * P])
        merged = sb("merged", [P, KD, NT])
        qd = merged[:, 0:2, :].rearrange("p a b -> p (a b)").rearrange("p (h i) -> p h i", h=RH)
        kd = merged[:, 2:GROUP, :].rearrange("p a b -> p (a b)")
        qT = merged[:, 0:GROUP, :]
        swish = merged[:, GROUP:, :].rearrange("p a b -> p (a b)").rearrange("p (t n) -> p t n", t=TILES)
        kept_scores = merged[:, :, :].rearrange("p a b -> p (a b)").rearrange("p (h a n) -> p h a n", h=PH, a=2)
        onehot = pick8k[:, 0, :].rearrange("p (s a) -> p s a", a=TOPK)
        queryT = attnT[:, 0:2, :]
        small = sb("small", [P, 32])
        stats = sb("stats", [P, RH, 6])
        mv = sb("mv", [P, RH, 2])
        rstd = sb("rstd", [P, RH])
        variance = sb("variance", [P, RH])
        roottmp = sb("roottmp", [P, RH])
        rest = vr[:, 0, :].rearrange("p (a c) -> p a c", a=2)
        val = maskedT[:, 0:2 * SLOTS].rearrange("p (a h k) -> p a h k", a=2, h=PH)
        idx = maskedT[:, 2 * SLOTS:].bitcast(U32).rearrange("p (a h k) -> p a h k", a=2, h=PH)
        topv = ret[:, 0:SLOTS].rearrange("p (h k) -> p h k", h=PH)
        topp = ret[:, SLOTS:2 * SLOTS].bitcast(U32)
        part_e, posu, posf, idxf = (ret[:, 2 * SLOTS + i * 2 * QUARTER:2 * SLOTS + (i + 1) * 2 * QUARTER].rearrange(
            "p (a s) -> p a s", a=2) for i in range(4))
        posu = posu.bitcast(U32)
        gsum = sb("gsum", [P, 2, PH])
        expert = sb("expert", [P, TILES, SLOTS], U32)
        gate = sb("gate", [P, TILES, SLOTS])
        x1 = sb("x1", [P, TILES, D])
        hdot = sb("hdot", [P, DEPTH, PAIR])
        hact = sb("hact", [P, DEPTH, PAIR])
        diag = sb("diag", [P, 2, PAIR, P])
        fstats = sb("fstats", [P, 2, 6])
        fmv = sb("fmv", [P, 2])
        frstd = sb("frstd", [P, 1])

        const_landed, par_landed, keys_landed = sem("const_landed"), sem("par_landed"), sem("keys_landed")
        landed = [sem(f"weights_landed{b}") for b in range(WRING)]
        kept_landed = [sem(f"kept_weights_landed{n}") for n in range(KEPT)]
        xT_landed, xn_landed = sem("xT_landed"), sem("xn_landed")
        bank_full = sem("bank_full")
        emptied = [sem(f"bank_emptied{b}") for b in range(BANKS)]
        state_zeroed = sem("state_zeroed")
        max_ready, exp_done, probs_ready = sem("max_ready"), sem("exp_done"), sem("probs_ready")
        scores_kept = sem("scores_kept")
        qd_ready, ret_ready, x1_ready = sem("qd_ready"), sem("ret_ready"), sem("x1_ready")
        gdiff_ready, gexp_done = sem("gdiff_ready"), sem("gate_exp_done")
        swish_tanh = sem("swish_tanh")
        mix_step, fin_step = sem("mix_step"), sem("fin_step")
        experts_published = sem("experts_published")
        published = sem("published")
        gathered = [sem(f"gathered{b}") for b in range(RING)]
        dots_done, gelu_done, gated, diag_ready = sem("dots_done"), sem("gelu_done"), sem("gated"), sem("diag_ready")
        up_done, acc_read = sem("up_done"), sem("acc_read")
        out_ready, stored = sem("out_ready"), sem("stored")
        passed = [sem("vector_passed"), sem("pool_passed")]
        pool_engine = nc.gpsimd

        def at(b, per, n):
            return b * per + n

        def started(b):
            return not isinstance(b, int) or b > 0

        def filled(b, *use):
            return at(b, len(USES), USE_AT[use] + 1)

        def bank_no(*use):
            return USE_AT[use] % BANKS

        def bank_of(*use):
            return ps[:, bank_no(*use), :]

        def free(b, *use):
            return at(b, BANK_USES[bank_no(*use)], USE_AT[use] // BANKS + 1)

        def stands(b, *uses, before=None):
            last = {bank_no(*u): u for u in sorted(uses, key=USE_AT.get)}
            return [(emptied[n], free(b, *u) + 1) for n, u in last.items() if before is None or n != bank_no(*before)]

        def buffer(g, i):
            return PLACE[g] * PAIR + i

        def arrived(b, g):
            return at(b, 16 * PLACE.count(PLACE[g]), 16 * PLACE[:g + 1].count(PLACE[g]))

        def used_before(b, g):
            n = max([m for m in range(g) if PLACE[m] == PLACE[g]], default=None)
            if n is None:
                return at(b, GROUPS, max(m for m in range(GROUPS) if PLACE[m] == PLACE[g]) + 1 - GROUPS) if started(b) else None
            return at(b, GROUPS, n + 1)

        def settle(eng):
            eng.sem_inc(passed[eng is pool_engine], 1)

        def spread(g, mix, done, ahead=False):
            share = EFFORT[-1] * (g - TAIL_END + 1) / (MIX_END - TAIL_END)
            goal = sum(effort <= share for effort in EFFORT)
            if ahead:
                goal = max(goal, min(AHEAD, (g - TAIL_END) // 2 + AHEAD + 1))
            while done[0] < goal:
                next(mix)
                done[0] += 1

        block = ctx.enter_context(nc.Block())

        @block.sync
        def _(sp):
            def loads(b):
                if started(b):
                    sp.wait_ge(bank_full, at(b, len(USES), 0))
                sp.dma_start(xT[:, :, :], xT_d[bass.ds(b, 1)].rearrange("b p k n -> (b p) k n")).then_inc(xT_landed, 16)
                if isinstance(b, int):
                    for n in range(KEPT):
                        sp.dma_start(kept_weights[:, n].rearrange("p u k c -> p (u k c)"), w_d[n]).then_inc(kept_landed[n], 16)
                        if n == 0:
                            sp.dma_start(const[:, :], const_d).then_inc(const_landed, 16)
                for n, pair in enumerate(STREAM):
                    if n >= WRING:
                        sp.wait_ge(bank_full, at(b, len(USES), LAST_USE[n - WRING] + 1))
                    elif started(b):
                        last = max(m for m in range(len(STREAM)) if m % WRING == n)
                        sp.wait_ge(bank_full, at(b - 1, len(USES), LAST_USE[last] + 1))
                    sp.dma_start(weights[:, n % WRING].rearrange("p u k c -> p (u k c)"),
                                 w_d[KEPT + n]).then_inc(landed[n % WRING], 16)
                    if isinstance(b, int) and n == WRING - 1:
                        sp.dma_start(par[:, :], par_d).then_inc(par_landed, 16)
                        sp.dma_start(keys[:, :, :], keys_d).then_inc(keys_landed, 16)
                    if pair == ("gate", 5):
                        sp.wait_ge(bank_full, filled(b, "ret_turn", 1, 0))
                        sp.dma_start(x1n[:, :, :],
                                     xn_d[bass.ds(b, 1)].rearrange("b p t d -> (b p) t d")).then_inc(xn_landed, 16)

            loads(0)
            with sp.Fori(1, BLOCKS) as b:
                loads(b)

        @block.gpsimd
        def _(pool):
            def gathers(b):
                for g in range(GROUPS):
                    t, s0 = g // TGROUPS, (g % TGROUPS) * PAIR
                    if g % TGROUPS == 0:
                        pool.wait_ge(experts_published, at(b, TILES, t + 1))
                    if used_before(b, g) is not None:
                        pool.wait_ge(up_done, used_before(b, g))
                        settle(pool)
                    for i in range(PAIR):
                        buf = buffer(g, i)
                        pool.indirect_dma_start(
                            out=rows[:, buf].rearrange("p a d -> p (a d)"), out_offset=None, in_=rows_d,
                            in_offset=bass.IndirectOffsetOnAxis(ap=expert[:, t, s0 + i:s0 + i + 1], axis=0),
                        ).then_inc(gathered[buf], 16)

            gathers(0)
            with pool.Fori(1, BLOCKS) as b:
                gathers(b)

        @block.scalar
        def _(act):
            def copy(out, use, b, scale=1.0, part=None):
                act.wait_ge(bank_full, filled(b, *use))
                bank = bank_of(*use)
                act.activation(out, bank if part is None else bank[part], ACT.Copy, scale=scale).then_inc(emptied[bank_no(*use)], 1)

            def mixer(b, parts=PARTS):
                for part in parts:
                    kind, *pos = part
                    if kind == "qa":
                        i = pos[0]
                        if i == 0 and started(b):
                            act.wait_ge(published, at(b, TILES, 0))
                        copy(qT[:, 2 * i:2 * i + 2, :].rearrange("p j n -> p (j n)"), (*part, 0), b, HD ** -0.5)
                    elif kind in ("qr", "kr"):
                        i = pos[0]
                        to = qrT if kind == "qr" else krT
                        copy(to[:, 2 * i:2 * i + 2, :].rearrange("p j n -> p (j n)"), (*part, 0), b,
                             P ** -0.5 if kind == "qr" else 1.0)
                    elif kind == "scores":
                        c, h = pos
                        n = c * KVH + h
                        lo = P if isinstance(b, int) and b == 0 and c == 0 else 0
                        act.wait_ge(max_ready, at(b, 2 * KVH, n + 1))
                        for j in range(GROUP):
                            act.activation(probs[:, j, lo:], probs[:, j, lo:], ACT.Exp, bias=small[:, 4 + j:5 + j],
                                           accum_out=small[:, 12 + j:13 + j])
                        act.activation(small[:, 16:20], small[:, 8:12], ACT.Exp).then_inc(exp_done, 1)
                    elif kind == "turn":
                        c, h = pos
                        for k in range(2):
                            copy(probsT[:, k, :], (*part, k), b)
                    elif kind == "pv":
                        c, h = pos
                        half = slice(HD * h, HD * h + HD)
                        act.wait_ge(bank_full, filled(b, *part, 0))
                        bank = bank_of(*part, 0)
                        act.activation(attnT[half, :, c * P:c * P + P],
                                             bank[half].rearrange("p (j n) -> p j n", j=GROUP), ACT.Copy, scale=0.5).then_inc(emptied[bank_no(*part, 0)], 1)
                    elif kind in ("gr", "gate"):
                        n = pos[0]
                        act.wait_ge(bank_full, filled(b, *part, 0))
                        bank = bank_of(*part, 0)
                        if kind == "gate":
                            for bank_emptied, turn in stands(b, ("branch", n - 2, 0) if n >= 2 else ("gr", n, 0)):
                                act.wait_ge(bank_emptied, turn)
                        elif started(b):
                            for bank_emptied, turn in stands(b - 1, ("branch", KD - 2 + n, 0)):
                                act.wait_ge(bank_emptied, turn)
                        ins = act.activation(gates[:, n % 2].rearrange("p a n -> p (a n)"), bank, ACT.Tanh, scale=0.5)
                        if kind == "gate":
                            ins.then_inc(emptied[bank_no(*part, 0)], 1)
                        else:
                            ins.then_inc(swish_tanh, 1)
                    elif kind == "ret_turn":
                        c = pos[0]
                        act.wait_ge(bank_full, filled(b, *part, 0))
                        bank = bank_of(*part, 0)
                        act.activation(retT[:, :, c * P:c * P + P],
                                             bank.rearrange("p (h n) -> p h n", h=RH), ACT.Copy, scale=0.25).then_inc(emptied[bank_no(*part, 0)], 1)
                    elif kind == "x1turn":
                        t = pos[0]
                        for i in range(2):
                            act.wait_ge(bank_full, filled(b, *part, i))
                            bank = bank_of(*part, i)
                            act.activation(xT[:, 4 * i:4 * i + 4, t * P:t * P + P],
                                                 bank.rearrange("p (k n) -> p k n", k=4), ACT.Copy).then_inc(emptied[bank_no(*part, i)], 1)
                    elif kind == "halves":
                        h = pos[0]
                        act.wait_ge(bank_full, filled(b, *part, 0))
                        bank = bank_of(*part, 0)
                        act.activation(kept_scores[:, h].rearrange("p a n -> p (a n)"), bank[:, 2 * NK:], ACT.Copy).then_inc(scores_kept, 1)
                    elif kind == "query":
                        copy(queryT[:, :, :].rearrange("p a n -> p (a n)"), (*part, 0), b)
                    elif kind == "softmax":
                        t = pos[0]
                        act.wait_ge(gdiff_ready, at(b, TILES, t + 1))
                        act.activation(topv[:, :, :], topv[:, :, :], ACT.Exp).then_inc(gexp_done, 1)
                    yield

            def weigh(b, g):
                t, s0 = g // TGROUPS, (g % TGROUPS) * PAIR
                act.wait_ge(dots_done, at(b, GROUPS, g + 1))
                act.activation(hact[:, g % DEPTH, :], hdot[:, g % DEPTH, :], ACT.Gelu).then_inc(gelu_done, 1)
                act.wait_ge(gelu_done, at(b, GROUPS, g + 1))
                for i in range(PAIR):
                    ins = act.activation(hact[:, g % DEPTH, i:i + 1], hact[:, g % DEPTH, i:i + 1], ACT.Copy,
                                         scale=gate[:, t, s0 + i:s0 + i + 1])
                ins.then_inc(gated, 1)
                act.wait_ge(gated, at(b, GROUPS, g + 1))
                if g > 1 or started(b):
                    act.wait_ge(up_done, at(b, GROUPS, g - 1))
                for i in range(PAIR):
                    ins = act.activation(diag[:, g % 2, i, :], ident, ACT.Copy, scale=hact[:, g % DEPTH, i:i + 1])
                ins.then_inc(diag_ready, 1)

            def head(b):
                for g in range(HEAD):
                    weigh(b, g)
                if started(b):
                    store(b - 1, 1)

            def body(b, mix):
                done = [0]
                tail = mixer(b, TAIL)
                for g in range(HEAD, GROUPS):
                    weigh(b, g)
                    if g in TAIL_AT:
                        next(tail)
                    if mix:
                        spread(g, mix, done)
                    if g == TGROUPS + 13:
                        store(b, 0)

            def store(b, t):
                act.wait_ge(out_ready, at(b, TILES, t + 1))
                act.dma_start(out_d[bass.ds(b, 1), t].rearrange("b p d -> (b p) d"), x1[:, t, :]).then_inc(stored, 16)

            act.wait_ge(const_landed, 16)
            for _ in mixer(0):
                pass
            head(0)
            with act.Fori(0, BLOCKS - 1) as b:
                body(b, mixer(b + 1))
                head(b + 1)
            body(BLOCKS - 1, None)
            store(BLOCKS - 1, 1)
            act.wait_ge(stored, 16 * TILES * BLOCKS)

        @block.tensor
        def _(pe):
            def mixer(b, parts=PARTS):
                for part in parts:
                    kind, *pos = part
                    if part in PAIR_AT:
                        n = PAIR_AT[part] - KEPT
                        if n < 0:
                            if isinstance(b, int):
                                pe.wait_ge(kept_landed[n + KEPT], 16)
                            w = kept_weights[:, n + KEPT]
                        else:
                            if kind != "branch" or pos[0] % 2 == 0:
                                pe.wait_ge(landed[n % WRING], at(b, 16 * BUF_PAIRS[n % WRING], 16 * (n // WRING + 1)))
                            w = weights[:, n % WRING]
                    if part == ("kv",):
                        pe.wait_ge(xT_landed, at(b, 16, 16))
                    if isinstance(b, int) and part == ("turn", 0, 0):
                        pe.wait_ge(const_landed, 16)
                    if isinstance(b, int) and part == ("halves", 0):
                        pe.wait_ge(keys_landed, 16)
                    last = None
                    if kind in ("qa", "qr", "kr", "gate", "query", "kv", "vr", "gr"):
                        if part == ("query", 0):
                            for bank_emptied, turn in stands(b, *(("x1turn", t, i) for t in range(TILES) for i in range(2)), before=(*part, 0)):
                                pe.wait_ge(bank_emptied, turn)
                        pe.wait_ge(emptied[bank_no(*part, 0)], free(b, *part, 0))
                        bank = bank_of(*part, 0)
                        for u in range(2):
                            if kind in ("vr", "gr") or (kind == "kv" and u == 1):
                                for t in range(TILES):
                                    at_col = TILES + t if kind == "kv" else t * 2 + u
                                    o = bank[:, at_col * P:(at_col + 1) * P]
                                    for k in range(KD):
                                        last = pe.matmul(o, xT[:, k, t * P:t * P + P], w[:, u, k, :],
                                                         start=k == 0, stop=k == KD - 1)
                            else:
                                for k in range(KD):
                                    last = pe.matmul(bank[:, u * NT:u * NT + NT], w[:, u, k, :], xT[:, k, :],
                                                     start=k == 0, stop=k == KD - 1)
                        last.then_inc(bank_full, 1)
                    elif kind == "scores":
                        c, h = pos
                        if part == ("scores", 0, 0):
                            for bank_emptied, turn in stands(b, ("kv", 0), ("qa", 0, 0), ("qa", 1, 0), before=(*part, 0)):
                                pe.wait_ge(bank_emptied, turn)
                        half = slice(HD * h, HD * h + HD)
                        for i in range(2):
                            pe.wait_ge(emptied[bank_no(*part, i)], free(b, *part, i))
                            bank = bank_of(*part, i)
                            for j in range(2):
                                last = pe.matmul(bank[:, j * NT:(j + 1) * NT], qT[half, 2 * i + j, c * P:c * P + P],
                                                 kT[half, c:c + 2, :].rearrange("p a n -> p (a n)"),
                                                 start=True, stop=True)
                            last.then_inc(bank_full, 1)
                    elif kind == "turn":
                        c, h = pos
                        pe.wait_ge(probs_ready, at(b, 2 * KVH, c * KVH + h + 1))
                        for k in range(2):
                            pe.wait_ge(emptied[bank_no(*part, k)], free(b, *part, k))
                            bank = bank_of(*part, k)
                            for j in range(GROUP):
                                last = pe.transpose(bank[:, j * P:j * P + P], probs[:, j, k * P:k * P + P], ident)
                            last.then_inc(bank_full, 1)
                    elif kind == "pv":
                        c, h = pos
                        half = slice(HD * h, HD * h + HD)
                        for bank_emptied, turn in stands(b, ("turn", c, h, 0), ("turn", c, h, 1), before=(*part, 0)):
                            pe.wait_ge(bank_emptied, turn)
                        pe.wait_ge(emptied[bank_no(*part, 0)], free(b, *part, 0))
                        bank = bank_of(*part, 0)
                        for k in range(2):
                            last = pe.matmul(bank[half], v[:, c + k, half], probsT[:, k, :],
                                             start=k == 0, stop=k == 1)
                        last.then_inc(bank_full, 1)
                    elif kind == "ret_scores":
                        c = pos[0]
                        if c == 0:
                            for bank_emptied, turn in stands(b, *((m, i, 0) for m in ("qr", "kr") for i in range(2)), before=(*part, 0)):
                                pe.wait_ge(bank_emptied, turn)
                        tok = slice(c * P, c * P + P)
                        pe.wait_ge(emptied[bank_no(*part, 0)], free(b, *part, 0))
                        bank = bank_of(*part, 0)
                        for h in range(RH):
                            last = pe.matmul(bank[:, h * P:h * P + P], krT[:, h, tok], qrT[:, h, tok],
                                             start=True, stop=True)
                        last.then_inc(bank_full, 1)
                        pe.wait_ge(emptied[bank_no(*part, 1)], free(b, *part, 1))
                        bank = bank_of(*part, 1)
                        for h in range(RH):
                            last = pe.transpose(bank[:, h * P:h * P + P], krT[:, h, tok], ident)
                        last.then_inc(bank_full, 1)
                    elif kind == "ret_out":
                        c = pos[0]
                        if isinstance(b, int) and c == 0:
                            pe.wait_ge(state_zeroed, 1)
                        for bank_emptied, turn in stands(b, *((("vr", 0, 0), ("vr", 1, 0)) if c == 0 else (("ret_out", 0, 1),)), ("ret_scores", c, 0), ("ret_scores", c, 1), before=(*part, 0)):
                            pe.wait_ge(bank_emptied, turn)
                        pe.wait_ge(qd_ready, at(b, TILES, c + 1))
                        pe.wait_ge(emptied[bank_no(*part, 0)], free(b, *part, 0))
                        bank = bank_of(*part, 0)
                        for h in range(RH):
                            o = slice(h * P, h * P + P)
                            pe.matmul(bank[:, o], maskedT[:, o], vr[:, c, o], start=True, stop=False)
                            last = pe.matmul(bank[:, o], qd[:, h, :], state[:, o], start=False, stop=True)
                        last.then_inc(bank_full, 1)
                        pe.wait_ge(emptied[bank_no(*part, 1)], free(b, *part, 1))
                        bank = bank_of(*part, 1)
                        for h in range(RH):
                            o = slice(h * P, h * P + P)
                            last = pe.matmul(bank[:, o], kd[:, o], vr[:, c, o], start=True, stop=True)
                        last.then_inc(bank_full, 1)
                    elif kind == "ret_turn":
                        c = pos[0]
                        pe.wait_ge(ret_ready, at(b, TILES, c + 1))
                        pe.wait_ge(emptied[bank_no(*part, 0)], free(b, *part, 0))
                        bank = bank_of(*part, 0)
                        for h in range(RH):
                            last = pe.transpose(bank[:, h * P:h * P + P], ret[:, h * P:h * P + P], ident)
                        last.then_inc(bank_full, 1)
                    elif kind == "branch":
                        m = pos[0]
                        if m == 0:
                            for bank_emptied, turn in stands(b, *(("pv", c, h, 0) for c in range(TILES) for h in range(KVH)), *(("ret_turn", c, 0) for c in range(TILES)), before=(*part, 0)):
                                pe.wait_ge(bank_emptied, turn)
                        pe.wait_ge(emptied[bank_no(*part, 0)], free(b, *part, 0))
                        bank = bank_of(*part, 0)
                        for side, src in enumerate((attnT, retT)):
                            for k in range(4):
                                last = pe.matmul(bank[:, side * NT:side * NT + NT], w[:, m % 2, side * 4 + k, :],
                                                 src[:, k, :], start=k == 0, stop=k == 3)
                        last.then_inc(bank_full, 1)
                    elif kind == "out":
                        if pos[0] == 0:
                            for bank_emptied, turn in stands(b, *(("branch", m, 0) for m in range(KD)), before=(*part, 0)):
                                pe.wait_ge(bank_emptied, turn)
                        pe.wait_ge(emptied[bank_no(*part, 0)], free(b, *part, 0))
                        bank = bank_of(*part, 0)
                        for u in range(2):
                            for t in range(TILES):
                                o = bank[:, (t * 2 + u) * P:(t * 2 + u + 1) * P]
                                for k in range(KD):
                                    last = pe.matmul(o, merged[:, k, t * P:t * P + P], w[:, u, k, :],
                                                     start=k == 0, stop=k == KD - 1)
                        last.then_inc(bank_full, 1)
                    elif kind == "x1turn":
                        t = pos[0]
                        pe.wait_ge(x1_ready, at(b, TILES, t + 1))
                        for i in range(2):
                            pe.wait_ge(emptied[bank_no(*part, i)], free(b, *part, i))
                            bank = bank_of(*part, i)
                            for k in range(4):
                                last = pe.transpose(bank[:, k * P:k * P + P],
                                                    x1n[:, t, (4 * i + k) * P:(4 * i + k + 1) * P], ident)
                            last.then_inc(bank_full, 1)
                    elif kind == "halves":
                        h = pos[0]
                        for bank_emptied, turn in stands(b, ("query", h, 0), before=(*part, 0)):
                            pe.wait_ge(bank_emptied, turn)
                        pe.wait_ge(emptied[bank_no(*part, 0)], free(b, *part, 0))
                        bank = bank_of(*part, 0)
                        for t in range(TILES):
                            for half in range(2):
                                last = pe.matmul(bank[:, (t * 2 + half) * P:(t * 2 + half + 1) * P],
                                                 queryT[:, half, t * P:t * P + P], keys[:, half, :],
                                                 start=True, stop=True)
                        last.then_inc(bank_full, 1)
                    yield

            def up(b, g):
                t, s0 = g // TGROUPS, (g % TGROUPS) * PAIR
                if g % TGROUPS == 0 and started(b):
                    pe.wait_ge(acc_read, at(b, TILES, t - 1))
                pe.wait_ge(diag_ready, at(b, GROUPS, g + 1))
                for i in range(PAIR):
                    buf = buffer(g, i)
                    for n in range(2):
                        last = pe.matmul(acc[:, t, n * 512:n * 512 + 512], diag[:, g % 2, i, :],
                                         rows[:, buf, 1, n * 512:n * 512 + 512],
                                         start=s0 + i == 0, stop=s0 + i == SLOTS - 1, skip_group_check=True)
                last.then_inc(up_done, 1)

            def head(b):
                if started(b):
                    up(b - 1, GROUPS - 1)
                for g in range(HEAD - 1):
                    up(b, g)

            def body(b, mix):
                done = [0]
                for g in range(HEAD, GROUPS):
                    if mix:
                        spread(g, mix, done, ahead=True)
                    up(b, g - 1)

            for _ in mixer(0):
                pass
            head(0)
            with pe.Fori(0, BLOCKS - 1) as b:
                body(b, mixer(b + 1))
                head(b + 1)
            body(BLOCKS - 1, None)
            up(BLOCKS - 1, GROUPS - 1)

        @block.vector
        def _(dve):
            def mixer(b, parts=PARTS):
                chain = 0 if parts is PARTS else MIX_STEPS

                def count():
                    nonlocal chain
                    chain += 1
                    return at(b, MIX_STEPS + TAIL_STEPS, chain)

                def top16(vals, ids, src, scratch):
                    dve.max(vals[:, 0:8], src).then_inc(mix_step, 1)
                    dve.wait_ge(mix_step, count())
                    settle(dve)
                    dve.max_index(ids[:, 0:8], vals[:, 0:8], src)
                    dve.match_replace(scratch, vals[:, 0:8], src, LOWEST).then_inc(mix_step, 1)
                    dve.wait_ge(mix_step, count())
                    settle(dve)
                    dve.max(vals[:, 8:16], scratch).then_inc(mix_step, 1)
                    dve.wait_ge(mix_step, count())
                    settle(dve)
                    return dve.max_index(ids[:, 8:16], vals[:, 8:16], scratch)

                def combine(h):
                    sums = cand[:, h % 2, :]
                    dve.tensor_tensor(sums.rearrange("p (i j) -> p i j", i=TOPK),
                                      val[:, 0, h].unsqueeze(2).to_broadcast([P, TOPK, TOPK]),
                                      val[:, 1, h].unsqueeze(1).to_broadcast([P, TOPK, TOPK]), ALU.add).then_inc(mix_step, 1)
                    dve.wait_ge(mix_step, count())
                    settle(dve)
                    top16(topv[:, h, :], topp[:, h * TOPK:(h + 1) * TOPK], sums, rest[:, 0, :]).then_inc(mix_step, 1)
                    dve.wait_ge(mix_step, count())
                    settle(dve)

                for part in parts:
                    kind, *pos = part
                    first = isinstance(b, int) and b == 0
                    if kind == "kv":
                        dve.wait_ge(bank_full, filled(b, *part, 0))
                        bank = bank_of(*part, 0)
                        dve.tensor_copy(kT[:, 0, :], kT[:, 2, :])
                        dve.tensor_copy(v[:, 0, :], v[:, 2, :]).then_inc(mix_step, 1)
                        dve.wait_ge(mix_step, count())
                        dve.tensor_copy(kT[:, 1:3, :].rearrange("p a n -> p (a n)"), bank[:, 0:NT])
                        dve.tensor_copy(v[:, 1:3, :].rearrange("p a n -> p (a n)"), bank[:, NT:]).then_inc(emptied[bank_no(*part, 0)], 1)
                    elif kind == "scores":
                        c, h = pos
                        lo = P if first and c == 0 else 0
                        if first and (c, h) == (0, 0):
                            dve.wait_ge(const_landed, 16)
                            dve.wait_ge(par_landed, 16)
                        for i in range(2):
                            dve.wait_ge(bank_full, filled(b, *part, i))
                            bank = bank_of(*part, i)
                            for j in range(2):
                                ins = dve.scalar_tensor_tensor(
                                    out=probs[:, 2 * i + j, lo:], in0=dist[:, lo:], scalar=-slopes[h * GROUP + 2 * i + j],
                                    in1=bank[:, j * NT + lo:(j + 1) * NT], op0=ALU.mult, op1=ALU.add)
                            ins.then_inc(emptied[bank_no(*part, i)], 1)
                        for bank_emptied, turn in stands(b, (*part, 0), (*part, 1)):
                            dve.wait_ge(bank_emptied, turn)
                        dve.tensor_reduce(small[:, 0:4], probs[:, :, lo:], AX, ALU.max).then_inc(mix_step, 1)
                        dve.wait_ge(mix_step, count())
                        sinks = par[:, R_SINK + h * GROUP:R_SINK + (h + 1) * GROUP]
                        dve.tensor_tensor(small[:, 0:4], small[:, 0:4], sinks, ALU.max).then_inc(mix_step, 1)
                        dve.wait_ge(mix_step, count())
                        dve.tensor_scalar(small[:, 4:8], small[:, 0:4], -1.0, None, ALU.mult)
                        dve.tensor_tensor(small[:, 8:12], sinks, small[:, 0:4], ALU.subtract).then_inc(max_ready, 1)
                    elif kind == "probs":
                        c, h = pos
                        lo = P if first and c == 0 else 0
                        dve.wait_ge(exp_done, at(b, 2 * KVH, c * KVH + h + 1))
                        dve.tensor_tensor(small[:, 20:24], small[:, 12:16], small[:, 16:20], ALU.add).then_inc(mix_step, 1)
                        dve.wait_ge(mix_step, count())
                        dve.reciprocal(small[:, 24:28], small[:, 20:24]).then_inc(mix_step, 1)
                        dve.wait_ge(mix_step, count())
                        for j in range(GROUP):
                            ins = dve.tensor_scalar(probs[:, j, lo:], probs[:, j, lo:], small[:, 24 + j:25 + j], None,
                                                    ALU.mult)
                        ins.then_inc(probs_ready, 1)
                    elif kind == "vr":
                        i = pos[0]
                        dve.wait_ge(bank_full, filled(b, *part, 0))
                        bank = bank_of(*part, 0)
                        dve.tensor_copy(vr[:, :, i * NT:i * NT + NT],
                                              bank.rearrange("p (t n) -> p t n", t=TILES)).then_inc(emptied[bank_no(*part, 0)], 1)
                    elif kind == "gr":
                        i = pos[0]
                        dve.wait_ge(bank_full, filled(b, *part, 0))
                        bank = bank_of(*part, 0)
                        e = gates[:, i % 2].rearrange("p a n -> p (a n)")
                        dve.wait_ge(swish_tanh, at(b, 2, i + 1))
                        dve.scalar_tensor_tensor(
                            out=swish[:, :, i * NT:i * NT + NT], in0=e.rearrange("p (t n) -> p t n", t=TILES), scalar=1.0,
                            in1=bank.rearrange("p (t n) -> p t n", t=TILES), op0=ALU.add, op1=ALU.mult).then_inc(mix_step, 1)
                        dve.wait_ge(mix_step, count())
                        gain = par[:, R_GN + i * NT:R_GN + i * NT + NT].unsqueeze(1).to_broadcast([P, TILES, NT])
                        dve.tensor_tensor(swish[:, :, i * NT:i * NT + NT], swish[:, :, i * NT:i * NT + NT],
                                                gain, ALU.mult).then_inc(emptied[bank_no(*part, 0)], 1)
                    elif kind == "ret_scores":
                        c = pos[0]
                        dve.wait_ge(bank_full, filled(b, *part, 0))
                        bank = bank_of(*part, 0)
                        dve.tensor_tensor(maskedT[:, :], bank, rmask, ALU.mult).then_inc(emptied[bank_no(*part, 0)], 1)
                        dve.wait_ge(bank_full, filled(b, *part, 1))
                        bank = bank_of(*part, 1)
                        dve.tensor_tensor(kd[:, :].rearrange("p (h n) -> p h n", h=RH),
                                                bank.rearrange("p (h n) -> p h n", h=RH),
                                                kdec.unsqueeze(2).to_broadcast([P, RH, P]), ALU.mult).then_inc(emptied[bank_no(*part, 1)], 1)
                        for bank_emptied, turn in stands(b, ("qr", 0, 0), ("qr", 1, 0)):
                            dve.wait_ge(bank_emptied, turn)
                        dve.tensor_tensor(qd[:, :, :], qrT[:, :, c * P:c * P + P], qdec, ALU.mult).then_inc(qd_ready, 1)
                    elif kind == "ret_out":
                        c = pos[0]
                        dve.wait_ge(bank_full, filled(b, *part, 0))
                        bank = bank_of(*part, 0)
                        for h in range(RH):
                            ins = dve.bn_stats(stats[:, h, :], bank[:, h * P:h * P + P])
                        ins.then_inc(mix_step, 1)
                        dve.wait_ge(mix_step, count())
                        settle(dve)
                        for h in range(RH):
                            ins = dve.bn_aggr(mv[:, h, :], stats[:, h, :])
                        ins.then_inc(mix_step, 1)
                        dve.wait_ge(mix_step, count())
                        dve.tensor_copy(variance[:, :], mv[:, :, 1]).then_inc(mix_step, 1)
                        dve.wait_ge(mix_step, count())
                        inverse_root(mix_step, count, rstd[:, :], variance[:, :], roottmp[:, :])
                        for h in range(RH):
                            ins = dve.tensor_scalar(ret[:, h * P:h * P + P], bank[:, h * P:h * P + P], mv[:, h, 0:1],
                                                    rstd[:, h:h + 1], ALU.subtract, ALU.mult)
                        ins.then_inc(emptied[bank_no(*part, 0)], 1)
                        for bank_emptied, turn in stands(b, (*part, 0), ("gr", 0, 0), ("gr", 1, 0)):
                            dve.wait_ge(bank_emptied, turn)
                        dve.tensor_tensor(ret[:, :], ret[:, :], swish[:, c, :], ALU.mult).then_inc(ret_ready, 1)
                        dve.wait_ge(bank_full, filled(b, *part, 1))
                        bank = bank_of(*part, 1)
                        for h in range(RH):
                            o = slice(h * P, h * P + P)
                            ins = dve.scalar_tensor_tensor(out=state[:, o], in0=state[:, o], scalar=chunk_decay[h],
                                                           in1=bank[:, o], op0=ALU.mult, op1=ALU.add)
                        ins.then_inc(emptied[bank_no(*part, 1)], 1)
                    elif kind == "branch":
                        m = pos[0]
                        dve.wait_ge(bank_full, filled(b, *part, 0))
                        bank = bank_of(*part, 0)
                        g = gates[:, m % 2].rearrange("p a n -> p (a n)")
                        for bank_emptied, turn in stands(b, ("gate", m, 0)):
                            dve.wait_ge(bank_emptied, turn)
                        dve.scalar_tensor_tensor(out=g, in0=g, scalar=1.0, in1=bank,
                                                 op0=ALU.add, op1=ALU.mult).then_inc(mix_step, 1)
                        dve.wait_ge(mix_step, count())
                        ins = dve.tensor_tensor(merged[:, m, :], g[:, 0:NT], g[:, NT:], ALU.add)
                        ins.then_inc(emptied[bank_no(*part, 0)], 1)
                    elif kind == "out":
                        n = pos[0]
                        if n == 0:
                            dve.wait_ge(xn_landed, at(b, 16, 16))
                        dve.wait_ge(bank_full, filled(b, *part, 0))
                        bank = bank_of(*part, 0)
                        to = x1n[:, :, n * NT:n * NT + NT]
                        dve.scalar_tensor_tensor(out=to, in0=to, scalar=ALPHA,
                                                       in1=bank.rearrange("p (t n) -> p t n", t=TILES),
                                                       op0=ALU.mult, op1=ALU.add).then_inc(emptied[bank_no(*part, 0)], 1)
                    elif kind == "norm":
                        t = pos[0]
                        if t == 0:
                            for bank_emptied, turn in stands(b, *(("out", n, 0) for n in range(4))):
                                dve.wait_ge(bank_emptied, turn)
                            for i in range(TILES):
                                for n in range(2):
                                    ins = dve.bn_stats(stats[:, 2 * i + n, :], x1n[:, i, n * 512:n * 512 + 512])
                            ins.then_inc(mix_step, 1)
                            dve.wait_ge(mix_step, count())
                            settle(dve)
                            for i in range(TILES):
                                ins = dve.bn_aggr(mv[:, i, :], stats[:, 2 * i:2 * i + 2, :].rearrange("p a s -> p (a s)"))
                            ins.then_inc(mix_step, 1)
                            dve.wait_ge(mix_step, count())
                            dve.tensor_copy(variance[:, 0:TILES], mv[:, 0:TILES, 1]).then_inc(mix_step, 1)
                            dve.wait_ge(mix_step, count())
                            inverse_root(mix_step, count, rstd[:, 0:TILES], variance[:, 0:TILES], roottmp[:, 0:TILES])
                        dve.tensor_scalar(x1n[:, t, :], x1n[:, t, :], mv[:, t, 0:1], rstd[:, t:t + 1],
                                          ALU.subtract, ALU.mult).then_inc(mix_step, 1)
                        dve.wait_ge(mix_step, count())
                        dve.tensor_tensor(x1n[:, t, :], x1n[:, t, :], par[:, R_MG:R_MB], ALU.mult).then_inc(mix_step, 1)
                        dve.wait_ge(mix_step, count())
                        dve.tensor_tensor(x1n[:, t, :], x1n[:, t, :], par[:, R_MB:R_FG], ALU.add).then_inc(x1_ready, 1)
                    elif kind == "halves":
                        h = pos[0]
                        dve.wait_ge(scores_kept, at(b, PH, h + 1))
                        bank = bank_of(*part, 0)
                        settle(dve)
                        for half in range(2):
                            ins = top16(val[:, half, h, :], idx[:, half, h, :],
                                        bank[:, half * NK:(half + 1) * NK], rest[:, half, 0:NK])
                        ins.then_inc(emptied[bank_no(*part, 0)], 1)
                        combine(h)
                    elif kind == "rank":
                        h = pos[0]
                        for half in range(2):
                            top16(val[:, half, h, :], idx[:, half, h, :], kept_scores[:, h, half, :],
                                  rest[:, half, 0:NK])
                        combine(h)
                    elif kind == "pick":
                        t, q = pos
                        slots = slice(q * QUARTER, (q + 1) * QUARTER)
                        dve.tensor_copy(idxf.rearrange("p a (h k) -> p a h k", h=2), idx[:, :, 2 * q:2 * q + 2, :])
                        dve.tensor_scalar(posu[:, 0, :], topp[:, slots], 4, None, ALU.logical_shift_right)
                        dve.tensor_scalar(posu[:, 1, :], topp[:, slots], TOPK - 1, None, ALU.bitwise_and).then_inc(mix_step, 1)
                        dve.wait_ge(mix_step, count())
                        dve.tensor_copy(posf, posu).then_inc(mix_step, 1)
                        dve.wait_ge(mix_step, count())
                        dve.tensor_tensor(onehot, posf.rearrange("p a s -> p (a s)").unsqueeze(2).to_broadcast([P, 2 * QUARTER, TOPK]),
                                          iota.unsqueeze(1).to_broadcast([P, 2 * QUARTER, TOPK]), ALU.is_equal).then_inc(mix_step, 1)
                        dve.wait_ge(mix_step, count())
                        hot = onehot.rearrange("p (h s) a -> p h s a", h=4)
                        ids = idxf.rearrange("p a (h k) -> p (a h) k", h=2)
                        dve.tensor_tensor(hot, hot, ids.unsqueeze(2).to_broadcast([P, 4, TOPK, TOPK]), ALU.mult).then_inc(mix_step, 1)
                        dve.wait_ge(mix_step, count())
                        dve.tensor_reduce(part_e.rearrange("p a s -> p (a s)"), onehot, AX, ALU.add).then_inc(mix_step, 1)
                        dve.wait_ge(mix_step, count())
                        ins = dve.scalar_tensor_tensor(out=expert[:, t, slots], in0=part_e[:, 0, :], scalar=float(NK),
                                                       in1=part_e[:, 1, :], op0=ALU.mult, op1=ALU.add)
                        if q == 3:
                            ins.then_inc(experts_published, 1)
                    elif kind == "softmax":
                        t = pos[0]
                        dve.tensor_copy(gsum[:, 0, :], topv[:, :, 0]).then_inc(mix_step, 1)
                        dve.wait_ge(mix_step, count())
                        dve.tensor_tensor(topv[:, :, :], topv[:, :, :],
                                          gsum[:, 0, :].unsqueeze(2).to_broadcast([P, PH, TOPK]),
                                          ALU.subtract).then_inc(gdiff_ready, 1)
                    elif kind == "gates":
                        t = pos[0]
                        dve.wait_ge(gexp_done, at(b, TILES, t + 1))
                        dve.tensor_reduce(gsum[:, 0, :], topv[:, :, :], AX, ALU.add).then_inc(mix_step, 1)
                        dve.wait_ge(mix_step, count())
                        dve.reciprocal(gsum[:, 1, :], gsum[:, 0, :]).then_inc(mix_step, 1)
                        dve.wait_ge(mix_step, count())
                        if started(b):
                            dve.wait_ge(diag_ready, at(b - 1, GROUPS, TGROUPS * (t + 1)))
                        dve.tensor_tensor(gate[:, t, :].rearrange("p (h k) -> p h k", h=PH), topv[:, :, :],
                                               gsum[:, 1, :].unsqueeze(2).to_broadcast([P, PH, TOPK]), ALU.mult).then_inc(mix_step, 1)
                        dve.wait_ge(mix_step, count())
                    elif kind == "publish":
                        publish(b, 0)
                    if part == parts[-1]:
                        assert chain == (MIX_STEPS if parts is PARTS else MIX_STEPS + TAIL_STEPS), chain
                    yield

            def inverse_root(step, count, out, var, tmp):
                dve.tensor_scalar(var, var, EPS, None, ALU.add).then_inc(step, 1)
                dve.wait_ge(step, count())
                dve.tensor_scalar(tmp.bitcast(U32), var.bitcast(U32), 1, None, ALU.logical_shift_right).then_inc(step, 1)
                dve.wait_ge(step, count())
                dve.tensor_scalar(out.bitcast(U32), tmp.bitcast(U32), -1.0, float(0x5F3759DF), ALU.mult, ALU.add).then_inc(step, 1)
                dve.wait_ge(step, count())
                for _ in range(3):
                    dve.scalar_tensor_tensor(out=tmp, in0=out, scalar=-0.5, in1=out, op0=ALU.mult, op1=ALU.mult).then_inc(step, 1)
                    dve.wait_ge(step, count())
                    dve.tensor_tensor(tmp, tmp, var, ALU.mult).then_inc(step, 1)
                    dve.wait_ge(step, count())
                    dve.scalar_tensor_tensor(out=out, in0=tmp, scalar=1.5, in1=out, op0=ALU.add, op1=ALU.mult).then_inc(step, 1)
                    dve.wait_ge(step, count())

            def publish(b, t):
                if started(b):
                    dve.wait_ge(stored, at(b - 1, 16 * TILES, 16 * (t + 1)))
                dve.tensor_copy(x1[:, t, :], x1n[:, t, :]).then_inc(published, 1)

            def finish(b, t):
                n, out = 0, x1[:, t, :]

                def count():
                    nonlocal n
                    n += 1
                    return at(b, FIN_STEPS * TILES, FIN_STEPS * t + n)

                dve.wait_ge(up_done, at(b, GROUPS, TGROUPS * (t + 1)))
                dve.scalar_tensor_tensor(out=out, in0=out, scalar=ALPHA, in1=acc[:, t, :],
                                         op0=ALU.mult, op1=ALU.add).then_inc(acc_read, 1)
                yield
                dve.wait_ge(acc_read, at(b, TILES, t + 1))
                for i in range(2):
                    ins = dve.bn_stats(fstats[:, i, :], out[:, i * 512:i * 512 + 512])
                ins.then_inc(fin_step, 1)
                dve.wait_ge(fin_step, count())
                settle(dve)
                dve.bn_aggr(fmv[:, :], fstats[:, :, :].rearrange("p a s -> p (a s)")).then_inc(fin_step, 1)
                dve.wait_ge(fin_step, count())
                inverse_root(fin_step, count, frstd[:, :], fmv[:, 1:2], roottmp[:, 0:1])
                yield
                dve.tensor_scalar(out, out, fmv[:, 0:1], frstd[:, 0:1], ALU.subtract, ALU.mult).then_inc(fin_step, 1)
                dve.wait_ge(fin_step, count())
                dve.tensor_tensor(out, out, par[:, R_FG:R_FB], ALU.mult).then_inc(fin_step, 1)
                dve.wait_ge(fin_step, count())
                dve.tensor_tensor(out, out, par[:, R_FB:R_GN], ALU.add).then_inc(out_ready, 1)
                assert n == FIN_STEPS
                yield

            MIX_STEPS, TAIL_STEPS, FIN_STEPS = 188, 112, 16

            def dots(b, g):
                t = g // TGROUPS
                if g % TGROUPS == 0:
                    dve.wait_ge(published, at(b, TILES, t + 1))
                if g >= DEPTH or started(b):
                    dve.wait_ge(gelu_done, at(b, GROUPS, g - DEPTH + 1))
                for i in range(PAIR):
                    buf = buffer(g, i)
                    dve.wait_ge(gathered[buf], arrived(b, g))
                    ins = dve.tensor_tensor_reduce(rows[:, buf, 0, :], rows[:, buf, 0, :], x1[:, t, :], 1.0, 0.0,
                                                   ALU.mult, ALU.add, hdot[:, g % DEPTH, i:i + 1])
                ins.then_inc(dots_done, 1)

            def head(b):
                output = finish(b - 1, 1) if started(b) else None
                for g in range(HEAD):
                    dots(b, g)
                    if output and 2 <= g <= 4:
                        next(output)

            def body(b, mix):
                done = [0]
                tail = mixer(b, TAIL)
                output = finish(b, 0)
                for g in range(HEAD, GROUPS):
                    dots(b, g)
                    if g in TAIL_AT:
                        next(tail)
                    if g == TAIL_END:
                        publish(b, 1)
                    if mix:
                        spread(g - 1, mix, done)
                    if g in (TGROUPS + 6, TGROUPS + 8, TGROUPS + 10):
                        next(output)

            for bank in range(BANKS):
                dve.sem_inc(emptied[bank], 1)
            dve.memset(small[:, :], 0.0)
            dve.memset(probs[:, :, :], 0.0)
            dve.memset(kT[:, 2, :], 0.0)
            dve.memset(v[:, 2, :], 0.0)
            dve.memset(state[:, :], 0.0).then_inc(state_zeroed, 1)
            dve.wait_ge(state_zeroed, 1)
            for _ in mixer(0):
                pass
            head(0)
            with dve.Fori(0, BLOCKS - 1) as b:
                body(b, mixer(b + 1))
                head(b + 1)
            body(BLOCKS - 1, None)
            for _ in finish(BLOCKS - 1, 1):
                pass


def kernel(**inputs):
    import numpy as _np
    import concourse.bacc as _bacc
    from concourse import mybir as _mybir
    from concourse.bass_utils import run_bass_kernel_spmd as _run

    a = {k: _np.asarray(v) for k, v in inputs.items()}
    x = a["x"][0]
    splits = _np.cumsum([0, AH * HD, KVH * HD, KVH * HD, RH * P, RH * P, RH * P, RH * P, D, D])
    qa, ka, va, qr, kr, vr, gr, ga, gb = (a["w_in"][0][:, splits[i]:splits[i + 1]] for i in range(9))

    def unit(w):
        return w.reshape(-1, P, P).transpose(1, 0, 2)

    heads = _np.concatenate([_np.r_[j * HD:(j + 1) * HD, (j + GROUP) * HD:(j + GROUP + 1) * HD] for j in range(GROUP)])
    qa = qa[:, heads]
    wa, wr = a["w_attn_branch"][0][heads], a["w_ret_branch"][0]
    wo, wq = a["w_out"][0], a["w_peer_query"][0]

    def col(w, n):
        return unit(w[:, n * P:(n + 1) * P])

    def pair(p):
        kind, i = p[0], p[1] if len(p) > 1 else 0
        if kind == "kv":
            return col(ka, 0), col(va, 0)
        if kind == "gate":
            return col(ga, i), col(gb, i)
        if kind == "branch":
            return tuple(_np.concatenate([col(wa, m), col(wr, m)], axis=1) for m in (i, i + 1))
        w = {"qa": qa, "qr": qr, "kr": kr, "vr": vr, "gr": gr, "out": wo, "query": wq}[kind]
        return col(w, 2 * i), col(w, 2 * i + 1)

    weights = _np.stack([_np.stack(pair(p), axis=1).reshape(P, 2 * D) for p in PAIRS])
    par = _np.concatenate([a[n][0] for n in ("ln_mix_gain", "ln_mix_bias", "ln_ffn_gain", "ln_ffn_bias",
                                             "ret_gn_gain", "attn_sinks")])
    arrays = {
        "xT_dram": x.T.reshape(KD, P, BLOCKS, NT).transpose(2, 1, 0, 3),
        "xn_dram": x.reshape(BLOCKS, TILES, P, D).transpose(0, 2, 1, 3),
        "weights_dram": weights,
        "keys_dram": a["peer_sub_keys"][0].transpose(2, 0, 1),
        "const_dram": constants(),
        "par_dram": _np.broadcast_to(par, (P, len(par))),
        "rows_dram": _np.concatenate([a["peer_down"][0], a["peer_up"][0]], axis=1),
    }
    arrays = {k: _np.ascontiguousarray(v) for k, v in arrays.items()}
    nc = _bacc.Bacc("TRN2", target_bir_lowering=False, num_devices=1)
    args = [nc.dram_tensor(k, v.shape, _mybir.dt.from_np(v.dtype), kind="ExternalInput").ap()
            for k, v in arrays.items()]
    out = nc.dram_tensor("out_dram", (BLOCKS, TILES, P, D), F32, kind="ExternalOutput").ap()
    build(nc, *args, out)
    r = _run(nc, [arrays], core_ids=[0])
    return r.results[0]["out_dram"].reshape(1, S, D)
```
